# Optimizing a Trainium2 kernel written in Bass

```python
import math
import jax, jax.numpy as jnp
from jax import lax
import numpy as np

D_MODEL = 2048
BATCH = 1
SEQ = 256
DEPTH = 1
DEC_BATCH = 8
DEC_SEQ = 1
PAST_LEN = 2048
PAGE_SIZE = 128

HEAD_DIM = 128
MIX_WIDTH = D_MODEL
NSA_WIDTH = MIX_WIDTH // 2
GDN_WIDTH = MIX_WIDTH - NSA_WIDTH
NSA_HEADS = NSA_WIDTH // HEAD_DIM
NSA_KV_HEADS = max(1, NSA_HEADS // 4)
NSA_GROUP = NSA_HEADS // NSA_KV_HEADS
KV_WIDTH = NSA_KV_HEADS * HEAD_DIM
CMP_BLOCK = 32
SEL_BLOCK = 64
CMP_PER_SEL = SEL_BLOCK // CMP_BLOCK
SEL_TOPN = 16
WINDOW = 512
NSA_Q_BLOCK = 64
CMP_HIDDEN = HEAD_DIM
GDN_HEADS = GDN_WIDTH // HEAD_DIM
CONV_WIDTH = 4
GDN_CHUNK = 64
PEER_HEADS = 8
PEER_NKEYS = 128
PEER_N_EXPERTS = PEER_NKEYS * PEER_NKEYS
PEER_QDIM = 256
PEER_TOPK = 16
PEER_BLOCK = 128
NORM_EPS = 1e-6
NEG_INF = -1e30
FORCE_SCORE = 1e4
IN_SPLITS = (NSA_WIDTH, 2 * KV_WIDTH, 2 * KV_WIDTH, 2 * KV_WIDTH, 3 * NSA_HEADS,
             3 * GDN_WIDTH, GDN_WIDTH, GDN_HEADS, GDN_HEADS)
IN_COLS = sum(IN_SPLITS)

kernel_name = 'hybrid_nsa_gdn_peer_adaln_step'

def rmsnorm(x, w):
    xf = x.astype(jnp.float32)
    y = xf * lax.rsqrt(jnp.mean(xf * xf, axis=-1, keepdims=True) + NORM_EPS)
    return (y * w.astype(jnp.float32)).astype(x.dtype)

def l2norm(x):
    return x * lax.rsqrt(jnp.sum(x * x, axis=-1, keepdims=True) + NORM_EPS)

def masked_softmax(s, mask, axis=-1):
    p = jax.nn.softmax(jnp.where(mask, s, NEG_INF), axis=axis)
    return jnp.where(mask, p, 0.0)

def alibi_slopes(n):
    return 2.0 ** (-8.0 * jnp.arange(1, n + 1, dtype=jnp.float32) / n)

def adaln(c, w, b):
    mod = jax.nn.silu(c) @ w + b
    return jnp.split(mod, 6, axis=-1)

def split_projection(p):
    B, T = p.shape[:2]
    offs = [int(o) for o in np.cumsum(IN_SPLITS)[:-1]]
    q, kvc, kvs, kvw, gts, qkv, z, bl, al = jnp.split(p, offs, axis=-1)
    kv_shape = (B, T, 2, NSA_KV_HEADS, HEAD_DIM)
    return (q.reshape(B, T, NSA_KV_HEADS, NSA_GROUP, HEAD_DIM), kvc.reshape(kv_shape),
            kvs.reshape(kv_shape), kvw.reshape(kv_shape),
            gts.reshape(B, T, NSA_KV_HEADS, NSA_GROUP, 3), qkv, z, bl, al)

def compress_blocks(kv, cmp_pe, cmp_w1, cmp_b1, cmp_w2):
    B, L = kv.shape[:2]
    nc = L // CMP_BLOCK
    blocks = kv[:, :nc * CMP_BLOCK].reshape(B, nc, CMP_BLOCK, 2, NSA_KV_HEADS, HEAD_DIM)
    blocks = blocks + jnp.transpose(cmp_pe, (1, 0, 2))[:, :, None, :]
    hid = jax.nn.gelu(jnp.einsum('bnlshd,slde->bnshe', blocks, cmp_w1) + cmp_b1[:, None, :])
    ckv = jnp.einsum('bnshe,sed->bnshd', hid, cmp_w2)
    cmp_end = jnp.arange(nc, dtype=jnp.int32) * CMP_BLOCK + (CMP_BLOCK - 1)
    return ckv, cmp_end

def selection_blocks(kv):
    B, L = kv.shape[:2]
    nsb = -(-L // SEL_BLOCK)
    kv = jnp.pad(kv, ((0, 0), (0, nsb * SEL_BLOCK - L), (0, 0), (0, 0), (0, 0)))
    kv = kv.reshape(B, nsb, SEL_BLOCK, 2, NSA_KV_HEADS, HEAD_DIM).transpose(3, 0, 4, 1, 2, 5)
    return kv[0], kv[1]

def nsa_attend(q, t_pos, gts, cmp_k, cmp_v, cmp_end, sel_k, sel_v, win_k, win_v, win_pos, slopes):
    f32 = jnp.float32
    B = q.shape[0]
    qf = q.astype(f32) * HEAD_DIM ** -0.5
    m = slopes[None, :, :, None, None]
    s = jnp.einsum('bqhgd,bnhd->bhgqn', qf, cmp_k.astype(f32))
    dist = (t_pos[:, None] - cmp_end[None, :]).astype(f32)
    p_cmp = masked_softmax(s - m * dist, cmp_end[None, :] <= t_pos[:, None])
    o_cmp = jnp.einsum('bhgqn,bnhd->bqhgd', p_cmp, cmp_v.astype(f32))
    nc = cmp_k.shape[1]
    nsb = sel_k.shape[2]
    imp = jnp.sum(p_cmp, axis=2)
    imp = jnp.pad(imp, ((0, 0), (0, 0), (0, 0), (0, nsb * CMP_PER_SEL - nc)))
    imp = imp.reshape(*imp.shape[:3], nsb, CMP_PER_SEL).sum(-1)
    blk = jnp.arange(nsb, dtype=jnp.int32)[None, :]
    cur = (t_pos // SEL_BLOCK)[:, None]
    forced = (blk == 0) | (blk == cur) | (blk == cur - 1)
    score = jnp.where(blk <= cur, jnp.where(forced, FORCE_SCORE, imp), NEG_INF)
    top_s, top_i = lax.top_k(score, min(SEL_TOPN, nsb))
    bi = jnp.arange(B)[:, None, None, None]
    hi = jnp.arange(NSA_KV_HEADS)[None, :, None, None]
    k_sel = sel_k[bi, hi, top_i].astype(f32)
    v_sel = sel_v[bi, hi, top_i].astype(f32)
    pos = top_i[..., None] * SEL_BLOCK + jnp.arange(SEL_BLOCK, dtype=jnp.int32)
    tq = t_pos[None, None, :, None, None]
    mask = ((top_s > 0.5 * NEG_INF)[..., None] & (pos <= tq))[:, :, None]
    dist = (tq - pos).astype(f32)[:, :, None]
    s = jnp.einsum('bqhgd,bhqnld->bhgqnl', qf, k_sel)
    p_sel = masked_softmax(s - m[..., None] * dist, mask, axis=(-2, -1))
    o_sel = jnp.einsum('bhgqnl,bhqnld->bqhgd', p_sel, v_sel)
    s = jnp.einsum('bqhgd,bkhd->bhgqk', qf, win_k.astype(f32))
    delta = t_pos[:, None] - win_pos[None, :]
    wmask = (delta >= 0) & (delta < WINDOW) & (win_pos[None, :] >= 0)
    p_win = masked_softmax(s - m * delta.astype(f32), wmask)
    o_win = jnp.einsum('bhgqk,bkhd->bqhgd', p_win, win_v.astype(f32))
    gate = jax.nn.sigmoid(gts.astype(f32))
    o = gate[..., 0:1] * o_cmp + gate[..., 1:2] * o_sel + gate[..., 2:3] * o_win
    return o.reshape(*q.shape[:2], NSA_WIDTH).astype(q.dtype)

def nsa_prompt(q, gts, kvc, kvs, kvw, cw, slopes):
    B, T = q.shape[:2]
    ckv, cmp_end = compress_blocks(kvc, *cw)
    sel_k, sel_v = selection_blocks(kvs)
    win = jnp.pad(kvw, ((0, 0), (WINDOW, 0), (0, 0), (0, 0), (0, 0)))
    nqb = T // NSA_Q_BLOCK
    qb = q.reshape(B, nqb, NSA_Q_BLOCK, *q.shape[2:]).swapaxes(0, 1)
    gb = gts.reshape(B, nqb, NSA_Q_BLOCK, *gts.shape[2:]).swapaxes(0, 1)

    def one_block(args):
        i, q_i, g_i = args
        start = i * NSA_Q_BLOCK
        t_pos = start + jnp.arange(NSA_Q_BLOCK, dtype=jnp.int32)
        w_i = lax.dynamic_slice_in_dim(win, start, WINDOW + NSA_Q_BLOCK, axis=1)
        w_pos = start - WINDOW + jnp.arange(WINDOW + NSA_Q_BLOCK, dtype=jnp.int32)
        return nsa_attend(q_i, t_pos, g_i, ckv[:, :, 0], ckv[:, :, 1], cmp_end, sel_k, sel_v,
                          w_i[:, :, 0], w_i[:, :, 1], w_pos, slopes)

    out = lax.map(one_block, (jnp.arange(nqb, dtype=jnp.int32), qb, gb))
    return out.swapaxes(0, 1).reshape(B, T, NSA_WIDTH)

def nsa_sample(q, gts, kvc, kvs, kvw, cache_cmp, cache_sel, page_table, win_buf, cw, slopes):
    Bd, Tn = q.shape[:2]
    past = page_table.shape[1] * PAGE_SIZE

    def with_past(cache, new):
        rows = cache[page_table].reshape(Bd, past, *cache.shape[2:])
        return jnp.concatenate([rows, new.astype(cache.dtype)], axis=1)

    ckv, cmp_end = compress_blocks(with_past(cache_cmp, kvc), *cw)
    sel_k, sel_v = selection_blocks(with_past(cache_sel, kvs))
    wkv = jnp.concatenate([win_buf, kvw.astype(win_buf.dtype)], axis=1)
    n_buf = win_buf.shape[1]
    t_pos = past + jnp.arange(Tn, dtype=jnp.int32)
    w_pos = past - n_buf + jnp.arange(n_buf + Tn, dtype=jnp.int32)
    o = nsa_attend(q, t_pos, gts, ckv[:, :, 0], ckv[:, :, 1], cmp_end, sel_k, sel_v,
                   wkv[:, :, 0], wkv[:, :, 1], w_pos, slopes)
    return o, wkv[:, Tn:]

def chunk_gated_delta(q, k, v, g, beta, s0):
    B, T, H, dk = q.shape
    dv = v.shape[-1]
    C = GDN_CHUNK
    n = -(-T // C)
    pad = n * C - T

    def chunks(a):
        a = jnp.pad(a, ((0, 0), (0, pad)) + ((0, 0),) * (a.ndim - 2))
        a = a.reshape(B, n, C, *a.shape[2:])
        return jnp.moveaxis(a, 3, 1)

    q, k, v, g, beta = (chunks(a) for a in (q, k, v, g, beta))
    G = jnp.cumsum(g, axis=-1)
    tri = jnp.tril(jnp.ones((C, C), bool))
    strict = jnp.tril(jnp.ones((C, C), bool), -1)
    diff = G[..., :, None] - G[..., None, :]
    decay = jnp.where(tri, jnp.exp(jnp.where(tri, diff, 0.0)), 0.0)
    kb = k * beta[..., None]
    A = jnp.einsum('bhncd,bhnmd->bhncm', kb, k) * jnp.where(strict, decay, 0.0)
    M = A + jnp.eye(C, dtype=A.dtype)
    rhs = jnp.concatenate([v * beta[..., None], kb * jnp.exp(G)[..., None]], axis=-1)
    sol = lax.linalg.triangular_solve(M, rhs, left_side=True, lower=True, unit_diagonal=True)
    U, W = sol[..., :dv], sol[..., dv:]
    qk = jnp.einsum('bhncd,bhnmd->bhncm', q, k) * decay
    qg = q * jnp.exp(G)[..., None]
    kd = k * jnp.exp(G[..., -1:] - G)[..., None]
    g_last = jnp.exp(G[..., -1])

    def step(S, xs):
        U_c, W_c, qk_c, qg_c, kd_c, gl_c = xs
        v_new = U_c - jnp.einsum('bhcd,bhde->bhce', W_c, S)
        o_c = jnp.einsum('bhcd,bhde->bhce', qg_c, S) + jnp.einsum('bhcm,bhme->bhce', qk_c, v_new)
        S = S * gl_c[..., None, None] + jnp.einsum('bhcd,bhce->bhde', kd_c, v_new)
        return S, o_c

    xs = tuple(jnp.moveaxis(a, 2, 0) for a in (U, W, qk, qg, kd, g_last))
    S, o = lax.scan(step, s0, xs)
    o = jnp.moveaxis(o, 0, 2).transpose(0, 2, 3, 1, 4).reshape(B, n * C, H, dv)[:, :T]
    return o, S

def gdn_mix(qkv, z, b_logit, a_logit, conv_buf, s0, conv_w, a_log, dt_bias, gn_w):
    f32 = jnp.float32
    B, T = qkv.shape[:2]
    xpad = jnp.concatenate([conv_buf.astype(qkv.dtype), qkv], axis=1)
    conv = sum(xpad[:, i:i + T] * conv_w[i] for i in range(CONV_WIDTH))
    conv = jax.nn.silu(conv.astype(f32))

    def heads(a):
        return a.reshape(B, T, GDN_HEADS, HEAD_DIM)

    q = l2norm(heads(conv[..., :GDN_WIDTH])) * HEAD_DIM ** -0.5
    k = l2norm(heads(conv[..., GDN_WIDTH:2 * GDN_WIDTH]))
    v = heads(conv[..., 2 * GDN_WIDTH:])
    beta = jax.nn.sigmoid(b_logit.astype(f32))
    g = -jnp.exp(a_log.astype(f32)) * jax.nn.softplus(a_logit.astype(f32) + dt_bias.astype(f32))
    o, s_new = chunk_gated_delta(q, k, v, g, beta, s0.astype(f32))
    o = rmsnorm(o, gn_w) * jax.nn.silu(heads(z).astype(f32))
    return o.reshape(B, T, GDN_WIDTH).astype(qkv.dtype), xpad[:, T:], s_new.astype(s0.dtype)

def peer_ffn(h, w_q, sub_keys, u_tab, v_tab):
    B, T, D = h.shape
    n = B * T
    nb = -(-n // PEER_BLOCK)
    flat = jnp.pad(h.reshape(n, D), ((0, nb * PEER_BLOCK - n), (0, 0))).reshape(nb, PEER_BLOCK, D)

    def one_block(hb):
        f32 = jnp.float32
        q = (hb @ w_q).astype(f32).reshape(PEER_BLOCK, PEER_HEADS, 2, PEER_QDIM // 2)
        s = jnp.einsum('nhpd,pkd->nhpk', q, sub_keys.astype(f32))
        s_half, i_half = lax.top_k(s, PEER_TOPK)
        cand = (s_half[:, :, 0, :, None] + s_half[:, :, 1, None, :]).reshape(PEER_BLOCK, PEER_HEADS, PEER_TOPK * PEER_TOPK)
        cid = (i_half[:, :, 0, :, None] * PEER_NKEYS + i_half[:, :, 1, None, :]).reshape(PEER_BLOCK, PEER_HEADS, PEER_TOPK * PEER_TOPK)
        best_s, best_j = lax.top_k(cand, PEER_TOPK)
        eid = jnp.take_along_axis(cid, best_j, axis=-1)
        gate = jax.nn.softmax(best_s, axis=-1)
        act = jax.nn.gelu(jnp.einsum('nd,nhkd->nhk', hb.astype(f32), u_tab[eid].astype(f32)))
        out = jnp.einsum('nhk,nhkd->nd', gate * act, v_tab[eid].astype(f32))
        return out.astype(hb.dtype)

    out = lax.map(one_block, flat)
    return out.reshape(nb * PEER_BLOCK, D)[:n].reshape(B, T, D)

def conditioned_layer(x, c, mixer, w_ada, b_ada, norm_mix, norm_ffn, w_in, w_out,
                      peer_wq, peer_keys, peer_u, peer_v):
    sh1, sc1, g1, sh2, sc2, g2 = adaln(c, w_ada, b_ada)
    h = rmsnorm(x, norm_mix) * (1.0 + sc1[:, None]) + sh1[:, None]
    mixed, states = mixer(split_projection(h @ w_in))
    x = x + g1[:, None] * (mixed @ w_out)
    h = rmsnorm(x, norm_ffn) * (1.0 + sc2[:, None]) + sh2[:, None]
    x = x + g2[:, None] * peer_ffn(h, peer_wq, peer_keys, peer_u, peer_v)
    return x, states

def stack_layers(per_layer, i):
    return jnp.stack([st[i] for st in per_layer])

def setup_inputs(seed: int = 0) -> dict:
    key = jax.random.key(seed)
    ks = iter(jax.random.split(key, 40))

    def nrm(shape, scale):
        return jax.random.normal(next(ks), shape, jnp.float32) * scale

    n_pages = PAST_LEN // PAGE_SIZE
    n_phys = (DEC_BATCH * n_pages * 5) // 4
    w_buf = min(WINDOW, PAST_LEN)
    row = (2, NSA_KV_HEADS, HEAD_DIM)
    page_table = jax.random.permutation(next(ks), n_phys)[:DEC_BATCH * n_pages].reshape(DEC_BATCH, n_pages).astype(jnp.int32)
    dt = jnp.exp(jax.random.uniform(next(ks), (DEPTH, GDN_HEADS), jnp.float32, minval=math.log(1e-3), maxval=math.log(1e-1)))
    a_init = jax.random.uniform(next(ks), (DEPTH, GDN_HEADS), jnp.float32, minval=1.0, maxval=16.0)
    return {
        'x_prompt': nrm((BATCH, SEQ, D_MODEL), 1.0),
        'x_sample': nrm((DEC_BATCH, DEC_SEQ, D_MODEL), 1.0),
        'cache_cmp_kv': nrm((DEPTH, n_phys, PAGE_SIZE) + row, 1.0),
        'cache_sel_kv': nrm((DEPTH, n_phys, PAGE_SIZE) + row, 1.0),
        'state_win_kv': nrm((DEPTH, DEC_BATCH, w_buf) + row, 1.0),
        'state_conv': nrm((DEPTH, DEC_BATCH, CONV_WIDTH - 1, 3 * GDN_WIDTH), 1.0),
        'state_gdn': nrm((DEPTH, DEC_BATCH, GDN_HEADS, HEAD_DIM, HEAD_DIM), 0.1),
        'page_table': page_table,
        'c_prompt': nrm((BATCH, D_MODEL), 1.0),
        'c_sample': nrm((DEC_BATCH, D_MODEL), 1.0),
        'w_ada': nrm((DEPTH, D_MODEL, 6 * D_MODEL), 0.5 * D_MODEL ** -0.5),
        'b_ada': nrm((DEPTH, 6 * D_MODEL), 0.01),
        'norm_mix': 1.0 + nrm((DEPTH, D_MODEL), 0.02),
        'norm_ffn': 1.0 + nrm((DEPTH, D_MODEL), 0.02),
        'w_in': nrm((DEPTH, D_MODEL, IN_COLS), D_MODEL ** -0.5),
        'cmp_pe': nrm((DEPTH, 2, CMP_BLOCK, HEAD_DIM), 0.02),
        'cmp_w1': nrm((DEPTH, 2, CMP_BLOCK, HEAD_DIM, CMP_HIDDEN), (CMP_BLOCK * HEAD_DIM) ** -0.5),
        'cmp_b1': nrm((DEPTH, 2, CMP_HIDDEN), 0.01),
        'cmp_w2': nrm((DEPTH, 2, CMP_HIDDEN, HEAD_DIM), CMP_HIDDEN ** -0.5),
        'conv_w': nrm((DEPTH, CONV_WIDTH, 3 * GDN_WIDTH), CONV_WIDTH ** -0.5),
        'gdn_a_log': jnp.log(a_init),
        'gdn_dt_bias': jnp.log(jnp.expm1(dt)),
        'gdn_norm': 1.0 + nrm((DEPTH, HEAD_DIM), 0.02),
        'w_out': nrm((DEPTH, D_MODEL, D_MODEL), D_MODEL ** -0.5),
        'peer_wq': nrm((DEPTH, D_MODEL, PEER_HEADS * PEER_QDIM), D_MODEL ** -0.5),
        'peer_keys': nrm((DEPTH, 2, PEER_NKEYS, PEER_QDIM // 2), (PEER_QDIM // 2) ** -0.5),
        'peer_u': nrm((DEPTH, PEER_N_EXPERTS, D_MODEL), D_MODEL ** -0.5),
        'peer_v': nrm((DEPTH, PEER_N_EXPERTS, D_MODEL), PEER_HEADS ** -0.5),
        'final_norm': 1.0 + nrm((D_MODEL,), 0.02),
    }

def reference(x_prompt, x_sample, cache_cmp_kv, cache_sel_kv, state_win_kv, state_conv, state_gdn,
              page_table, c_prompt, c_sample, w_ada, b_ada, norm_mix, norm_ffn, w_in, cmp_pe, cmp_w1,
              cmp_b1, cmp_w2, conv_w, gdn_a_log, gdn_dt_bias, gdn_norm, w_out, peer_wq, peer_keys,
              peer_u, peer_v, final_norm):
    slopes = alibi_slopes(NSA_HEADS).reshape(NSA_KV_HEADS, NSA_GROUP)
    xp, xs = x_prompt, x_sample
    prompt_states, sample_states = [], []
    for l in range(DEPTH):
        cw = (cmp_pe[l], cmp_w1[l], cmp_b1[l], cmp_w2[l])
        gw = (conv_w[l], gdn_a_log[l], gdn_dt_bias[l], gdn_norm[l])
        shared = (w_ada[l], b_ada[l], norm_mix[l], norm_ffn[l], w_in[l], w_out[l],
                  peer_wq[l], peer_keys[l], peer_u[l], peer_v[l])

        def prompt_mixer(parts):
            q, kvc, kvs, kvw, gts, qkv, z, bl, al = parts
            o_nsa = nsa_prompt(q, gts, kvc, kvs, kvw, cw, slopes)
            Bp, T = q.shape[:2]
            conv0 = jnp.zeros((Bp, CONV_WIDTH - 1, qkv.shape[-1]), qkv.dtype)
            s0 = jnp.zeros((Bp, GDN_HEADS, HEAD_DIM, HEAD_DIM), jnp.float32)
            o_gdn, conv_new, s_new = gdn_mix(qkv, z, bl, al, conv0, s0, *gw)
            keep = min(WINDOW, T)
            return jnp.concatenate([o_nsa, o_gdn], axis=-1), (kvc, kvs, kvw[:, T - keep:], conv_new, s_new)

        def sample_mixer(parts):
            q, kvc, kvs, kvw, gts, qkv, z, bl, al = parts
            o_nsa, win_new = nsa_sample(q, gts, kvc, kvs, kvw, cache_cmp_kv[l], cache_sel_kv[l],
                                        page_table, state_win_kv[l], cw, slopes)
            o_gdn, conv_new, s_new = gdn_mix(qkv, z, bl, al, state_conv[l], state_gdn[l], *gw)
            return jnp.concatenate([o_nsa, o_gdn], axis=-1), (kvc, kvs, win_new, conv_new, s_new)

        xp, st_p = conditioned_layer(xp, c_prompt, prompt_mixer, *shared)
        xs, st_s = conditioned_layer(xs, c_sample, sample_mixer, *shared)
        prompt_states.append(st_p)
        sample_states.append(st_s)
    y_prompt = rmsnorm(xp, final_norm)
    y_sample = rmsnorm(xs, final_norm)
    return (y_prompt, y_sample,
            stack_layers(prompt_states, 0), stack_layers(sample_states, 0),
            stack_layers(prompt_states, 1), stack_layers(sample_states, 1),
            stack_layers(prompt_states, 2), stack_layers(sample_states, 2),
            stack_layers(prompt_states, 3), stack_layers(sample_states, 3),
            stack_layers(prompt_states, 4), stack_layers(sample_states, 4))


_drawn_inputs = setup_inputs


def setup_inputs(seed=0):
    import zlib

    import numpy as np

    out = dict(_drawn_inputs(seed))
    spreads = {}
    factors = {'norm_ffn': 6.407, 'cmp_pe': 26.122, 'cmp_b1': 57.275, 'gdn_norm': 8.0, 'final_norm': 7.4}
    for name, (base, spread) in spreads.items():
        noise = np.random.default_rng([zlib.crc32(name.encode()), seed]).standard_normal(out[name].shape)
        drawn = base * np.exp(spread * noise) if base else spread * noise
        out[name] = __import__('jax').numpy.asarray(drawn.astype(out[name].dtype))
    for name, factor in factors.items():
        out[name] = (out[name] * factor).astype(out[name].dtype)
    return out
```

```python
from contextlib import ExitStack

import numpy as np
import concourse.bass as bass
from concourse import mybir
from concourse.alu_op_type import AluOpType as ALU

F32 = mybir.dt.float32
I32 = mybir.dt.int32
U32 = mybir.dt.uint32
ACT = mybir.ActivationFunctionType
AX = mybir.AxisListType.X

P = 128
D = 2048
KD = D // P
T = 256
NT = T // P
NB = 8
TC = T + NB
HD = 128
HEADS = 8
KVH = 2
PAIRS = NB * KVH
ROWS = NB * HEADS
PAST = 2048
PAGES = PAST // P
NPHYS = NB * PAGES * 5 // 4
CMP = 32
NC = PAST // CMP
NCP = T // CMP
SEL = 64
NSEL = PAST // SEL + 1
TOPN = 16
WIN = 512
EPS = 1e-6
BIG = 1e30
FORCE = 1e4
FAR = 1e32
SCALE = float(HD) ** -0.5
B_Q, B_CK, B_CV, B_SK, B_SV, B_WK, B_WV, B_GQ, B_GK, B_GV, B_Z, NBLK = 0, 8, 10, 12, 14, 16, 18, 20, 28, 36, 44, 52
COL_GATES = 2560
COL_G = COL_GATES + 24
COL_BA = COL_G + 32 * P
NKEYS = 128
TOPK = 16
SLOTS = HEADS * TOPK
SLOT = 4096
RING = 4
M_SH1, M_SC1, M_G1, M_SH2, M_SC2, M_G2 = (KD * i for i in range(6))

CLEARED = """
    page_T cond_T cond_ready x_blocks hid_bias_ready x_T hid_sum odd_moved
    cmp_sum hid_ready row_xor params_T x_moved params_ready hid_bias_sum mod_sum
    modrow_moved mod_moved cmp_moved params_moved even_moved ck_moved gates_fm gates_fm_moved
    gates_T gates_moved crows_moved crows_T state_T conv_silu conv_sum csilu
    z_ready qk_squares qk_sums qk_root beta_ready gates_ready sp_abs act_steps
    softplus log_decay decay_sums decay_left decay_exps sg_ready state_new delta_out
    decay_mm kk_mm decay_moved qk_mm rows_T q0_ready am_ready p0_T
    level_ready p0_ready qk_masked p_new y_mm y_moved rows_moved q_new
    py_mm yq_mm ks_mm r_ready vn_mm vn_moved qg_ready o_mm
    kd_ready s_mm vn_used q_scaled step_ready step_ks egb_ready vn_ready
    step_rows step_rows_moved outer vdiag_ready decayed outer_added o_root step_bc
""".split()
LATE = """
    win_copied hpart_clear kv_rows kv_out w2b_in kv_T cmpk_ready hpart_sum
    hpart_moved hidp_sum hidp_ready cmpp_sum cmpp_moved q_scaled_att score_read score_mm
    p_ready pt_moved pt_T o_moved o_mm_att states_done top_ready exp_done
    pt_part att_steps item_used samp_consts ranked pts_clear samp_steps samp_ready
    scmp_mm samp_top samp_exp pc_ready kt_T kt_used kt_even imp_mm
    picked_mm samp_p samp_pT samp_pt_dve samp_folded samp_mixed kt_odd samp_pt_act
    vnew_mm vnew_moved pv_mm pv_used pv_moved x1_ready top_steps keyscores
    top_diff best_exp experts_ready keys_in keys_T keys_ready keyscore_mm rows_mm
    rows_out spread_mm spread_diag spread g2_mm g2_rows experts_T peer_consts
    gather_turn idx_ready experts_s y_ready y_out peer_steps dot gelu
    summed x2_ready y_root gates_here v_used diag_ready h2_spread sumsq
""".split()


def layer_program(nc, io, outs):
    ctx = ExitStack()
    with ctx:
        sb = lambda name, shape, dt=F32: ctx.enter_context(nc.sbuf_tensor("sb_" + name, shape, dt))
        made = {}

        def sem(name):
            if name not in made:
                made[name] = sem(CLEARED[LATE.index(name)]) if name in LATE else ctx.enter_context(nc.semaphore(name))
            return made[name]

        ring = sb("ring", [P, RING, SLOT])
        xT = sb("xT", [P, KD * TC])
        hT = sb("hT", [P, KD * TC])
        pT = sb("pT", [P, NBLK * TC])
        work = sb("work", [P, 7168])
        modT = sb("modT", [P, 96 * 9])
        ckT = sb("ckT", [P, PAIRS * NC])
        cvR = sb("cvR", [NC, PAIRS * HD])
        ident = sb("ident", [P, P])
        ones = sb("ones", [P, P])
        upto = sb("upto", [P, P])
        above = sb("above", [P, P])
        levels = sb("levels", [P, 7 * P])
        dist = sb("dist", [P, NT * T])
        cdist = sb("cdist", [P, NT * NCP])
        cseen = sb("cseen", [P, NT * NCP])
        params = sb("params", [P, 3 * P])
        gt = sb("gt", [P, 3 * 40])
        small = sb("small", [P, 640])
        pagesb = sb("pagesb", [1, P], I32)
        ps = ctx.enter_context(nc.psum_tensor("ps", [P, 8, 512], F32))

        v3 = lambda t, off, a, b: t[:, off:off + a * b].rearrange("p (a b) -> p a b", b=b)
        v4 = lambda t, off, a, b, c: t[:, off:off + a * b * c].rearrange("p (a b c) -> p a b c", b=b, c=c)
        xT3, hT3, pT3 = v3(xT, 0, KD, TC), v3(hT, 0, KD, TC), v3(pT, 0, NBLK, TC)
        mod3 = v3(modT, 0, 96, 9)
        bias_ada = params[:, 0:96]
        conv_wT = params[:, P:P + 96]
        norm1T, norm2T = params[:, 2 * P:2 * P + 16], params[:, 2 * P + 16:2 * P + 32]
        finalT = params[:, 2 * P + 32:2 * P + 48]
        gnT = params[:, 2 * P + 48:2 * P + 49]
        cb1T = params[:, 2 * P + 49:2 * P + 51]
        peT = params[:, 2 * P + 51:2 * P + 115]
        SM = {}
        at = [0]

        def cols(name, n):
            SM[name] = small[:, at[0]:at[0] + n]
            at[0] += n
            assert at[0] <= 640
            return SM[name]

        hid_bias = cols("hid_bias", 2)
        eps_col = cols("eps_col", 1)
        fold = cols("fold", 96)
        w1 = pT[:, 0:2 * SLOT]
        XT = [pT[:, 2 * SLOT:3 * SLOT], hT[:, 0:SLOT]]
        w2 = work[:, 0:2 * HD]
        hid = [work[:, 256:384], work[:, 384:512]]
        cT = work[:, 512:512 + KD * 32]
        modrow = [work[:, 1536:1792], work[:, 1792:2048]]
        prow = work[:, 1024:1024 + 3 * P]
        crow = work[:, 1536:1536 + D]
        xrow = work[:, 3584:3584 + D]
        xrow2 = hT[:, D:2 * D]

        full = [sem(f"slot_full{j}") for j in range(RING)]
        out_sems = {}
        block = ctx.enter_context(nc.Block())

        n_static = {}

        def step(eng, s, ins, by=1):
            ins.then_inc(s, by)
            n_static[s] = n_static.get(s, 0) + by
            eng.wait_ge(s, n_static[s])

        def mark(s, ins, by=1):
            ins.then_inc(s, by)
            n_static[s] = n_static.get(s, 0) + by
            return n_static[s]

        ADA_ITEMS = 6

        def bank(i):
            return ps[:, i, :]


        def sp_compress(sp):
            sp.dma_start(pagesb[:], io["page_table"].rearrange("(a b) c -> a (b c)", a=1)).then_inc(sem("pages_in"), 16)
            for s in range(2):
                sp.dma_start(w1[:, s * SLOT:(s + 1) * SLOT].rearrange("p (l e) -> p l e", e=HD),
                             io["cmp_w1"][0, s].rearrange("l d e -> d l e")).then_inc(sem("w1_in"), 16)
            sp.wait_ge(sem("pages_in"), 16)
            wada = io["w_ada"][0].rearrange("(k p) n -> p k n", p=P)
            with sp.Fori(0, NB) as b:
                for half in range(2):
                    sp.wait_ge(sem("mod_part"), b * ADA_ITEMS + 3 + half)
                    for pp in range(8):
                        page = sp.value_load(pagesb[0:1, bass.ds(b * PAGES + (half * 8 + pp), 1)], min_val=0, max_val=NPHYS - 1)
                        sp.dma_start(ring[:, half, pp * 512:(pp + 1) * 512],
                                     io["cache_cmp_kv"][0, bass.ds(page, 1)].rearrange("a t s h d -> (a t) (s h d)")).then_inc(full[half], 16)
                for a in range(ADA_ITEMS):
                    j = (2 + a) % RING
                    if a in (2, 3):
                        sp.wait_ge(sem("page_T"), b * PAGES + 8 * (a - 1))
                    else:
                        sp.wait_ge(sem("mod_part"), b * ADA_ITEMS + (5 + a if a < 2 else 3 + a))
                    sp.dma_start(ring[:, j, :].rearrange("p (k n) -> p k n", k=KD),
                                 wada[:, :, bass.ds(b * (ADA_ITEMS * 256) + a * 256, 256)]).then_inc(full[j], 16)

        def act_setup(act):
            act.dma_start(prow[0:96, 0:P], io["b_ada"][0].rearrange("(a p) -> a p", p=P)).then_inc(sem("params_in"), 16)
            act.dma_start(prow[0:96, P:2 * P], io["conv_w"][0].rearrange("i (a p) -> (i a) p", p=P)).then_inc(sem("params_in"), 16)
            for i, name in enumerate(("norm_mix", "norm_ffn")):
                act.dma_start(prow[16 * i:16 * i + 16, 2 * P:3 * P], io[name][0].rearrange("(a p) -> a p", p=P)).then_inc(sem("params_in"), 16)
            act.dma_start(prow[32:48, 2 * P:3 * P], io["final_norm"].rearrange("(a p) -> a p", p=P)).then_inc(sem("params_in"), 16)
            act.dma_start(prow[48:49, 2 * P:3 * P], io["gdn_norm"]).then_inc(sem("params_in"), 16)
            act.dma_start(prow[49:51, 2 * P:3 * P], io["cmp_b1"][0]).then_inc(sem("params_in"), 16)
            act.dma_start(prow[51:115, 2 * P:3 * P], io["cmp_pe"][0].rearrange("s l d -> (s l) d")).then_inc(sem("params_in"), 16)
            act.dma_start(crow[0:1, :], io["c_prompt"]).then_inc(sem("cond_in"), 16)
            act.dma_start(crow[1:9, :], io["c_sample"]).then_inc(sem("cond_in"), 16)
            act.dma_start(w2.rearrange("p (s d) -> p s d", s=2), io["cmp_w2"][0].rearrange("s e d -> e s d")).then_inc(sem("w2_in"), 16)
            xp = io["x_prompt"][0].rearrange("(t p) d -> t p d", p=P)
            act.dma_start(xrow, xp[0]).then_inc(sem("x_in"), 16)
            act.dma_start(xrow2, xp[1]).then_inc(sem("x2_in"), 16)
            act.wait_ge(sem("cond_T"), 1)
            act.wait_ge(sem("consts"), 7)
            act.activation(v3(cT, 0, KD, 32)[:, :, 0:9], v3(bank(7), 0, KD, 32)[:, :, 0:9], ACT.Silu).then_inc(sem("cond_ready"), 1)
            act.wait_ge(sem("x_blocks"), 4)
            act.dma_start(xrow[0:NB, :], io["x_sample"].rearrange("b t d -> (b t) d")).then_inc(sem("xs_in"), 16)

        def act_compress(act):
            act.wait_ge(sem("hid_bias_ready"), 1)
            act.wait_ge(sem("x_T"), 2)
            with act.Fori(0, NB) as b:
                for pp in range(1, PAGES, 2):
                    act.wait_ge(sem("page_T"), b * PAGES + pp + 1)
                    if pp == 1:
                        act.wait_ge(sem("hid_sum"), b * 2 + 2)
                    for s in range(2):
                        mv = act.activation(XT[s].rearrange("p (l h n) -> p h n l", h=KVH, n=NC)[:, :, 4 * pp:4 * pp + 4, :],
                                            bank(1)[:, 256 * s:256 * s + 256].rearrange("p (h n l) -> p h n l", h=KVH, n=4),
                                            ACT.Copy)
                    mv.then_inc(sem("odd_moved"), 1)
                for s in range(2):
                    act.wait_ge(sem("hid_sum"), b * 2 + s + 3)
                    act.wait_ge(sem("cmp_sum"), b + 1)
                    act.activation(hid[s], bank(2 + s)[:, 0:P], ACT.Gelu_apprx_tanh,
                                   bias=hid_bias[:, s:s + 1]).then_inc(sem("hid_ready"), 1)

        def pool_setup(pool):
            pool.iota(work[:, 1408:1536].bitcast(I32), [[1, P]], base=0, channel_multiplier=0).then_inc(sem("row_xor"), 1)
            pool.iota(levels[:, 0:P].bitcast(I32), [[0, P]], base=0, channel_multiplier=1).then_inc(sem("row_xor"), 1)
            c = sem("consts")
            step(pool, c, pool.memset(ones[:], 1.0))
            step(pool, c, pool.affine_select(out=ident[:], in_=ones[:], compare_op=ALU.is_equal, fill=0.0, base=0,
                                             pattern=[[-1, P]], channel_multiplier=1))
            step(pool, c, pool.affine_select(out=upto[:], in_=ones[:], compare_op=ALU.is_ge, fill=0.0, base=0,
                                             pattern=[[1, P]], channel_multiplier=-1))
            step(pool, c, pool.affine_select(out=above[:], in_=ones[:], compare_op=ALU.is_gt, fill=0.0, base=0,
                                             pattern=[[-1, P]], channel_multiplier=1))
            step(pool, c, pool.memset(eps_col, EPS))
            step(pool, c, pool.memset(fold, 0.0))
            step(pool, c, pool.memset(cT, 0.0))
            for j in range(4):
                step(pool, c, pool.tensor_tensor(fold[:, 0:32], fold[:, 0:32], ident[:, 32 * j:32 * j + 32], ALU.add))
            step(pool, c, pool.memset(gt[:], 0.0))

        def pe_setup(pe):
            pe.wait_ge(sem("consts"), 2)
            pe.wait_ge(sem("params_in"), 16 * 8)
            for i, rows in enumerate((96, 96, 115)):
                mm = pe.transpose(bank(6)[:, i * P:i * P + rows], prow[0:rows, i * P:(i + 1) * P], ident[0:rows, 0:rows])
            mm.then_inc(sem("params_T"), 1)
            pe.wait_ge(sem("cond_in"), 32)
            for k in range(KD):
                mm = pe.transpose(bank(7)[:, k * 32:k * 32 + 9], crow[0:9, k * P:(k + 1) * P], ident[0:9, 0:9])
            mm.then_inc(sem("cond_T"), 1)
            n = 0
            for t, (row, rows, got) in enumerate(((xrow, P, "x_in"), (xrow2, P, "x2_in"), (xrow, NB, "xs_in"))):
                pe.wait_ge(sem(got), 16)
                for k4 in range(KD // 4):
                    if n >= 2:
                        pe.wait_ge(sem("x_moved"), n - 1)
                    for k in range(4):
                        mm = pe.transpose(bank(n % 2)[:, k * P:k * P + rows], row[0:rows, (4 * k4 + k) * P:(4 * k4 + k + 1) * P],
                                          ident[0:rows, 0:rows])
                    mm.then_inc(sem("x_blocks"), 1)
                    n += 1

        def pe_compress(pe):
            pe.wait_ge(sem("w1_in"), 32)
            pe.wait_ge(sem("params_ready"), 1)
            for s in range(2):
                for l in range(CMP):
                    mm = pe.matmul(bank(3)[:, s:s + 1], w1[:, (s * CMP + l) * HD:(s * CMP + l + 1) * HD],
                                   peT[:, s * CMP + l:s * CMP + l + 1], start=l == 0, stop=l == CMP - 1)
            mm.then_inc(sem("hid_bias_sum"), 1)
            pe.wait_ge(sem("cond_ready"), 1)
            pe.wait_ge(sem("x_moved"), 12)
            pe.wait_ge(sem("consts"), 11)
            pe.sem_inc(sem("mod_part"), ADA_ITEMS)
            pe.sem_inc(sem("mod_sum"), 2)
            pe.sem_inc(sem("hid_sum"), 2)
            pe.sem_inc(sem("cmp_sum"), 1)
            pe.wait_ge(sem("w2_in"), 16)

            with pe.Fori(0, NB) as b:
                for half in range(2):
                    pe.wait_ge(full[half], b * 144 + 128)
                    for q in range(8):
                        pp = half * 8 + q
                        pe.wait_ge(sem("odd_moved" if pp % 2 else "even_moved"), b * (PAGES // 2) + pp // 2 + 1)
                        for c in range(4):
                            mm = pe.transpose(bank(pp % 2)[:, c * P:(c + 1) * P],
                                              ring[:, half, q * 512 + c * P:q * 512 + (c + 1) * P], ident[:])
                        mm.then_inc(sem("page_T"), 1)

                def modulation(a):
                    j = (2 + a) % RING
                    pe.wait_ge(full[j], b * 144 + 144 if j < 2 else b * 32 + (16 if a < 2 else 32))
                    pe.wait_ge(sem("modrow_moved"), b * ADA_ITEMS + a + 1)
                    w = ring[:, j, :].rearrange("p (k n) -> p k n", k=KD)
                    for k4 in range(KD // 4):
                        for g in range(4):
                            k = 4 * k4 + g
                            mm = pe.matmul(bank(5 + a % 2)[32 * g:32 * g + 32, 0:256], cT[:, k * 32:k * 32 + 32],
                                           w[:, k, :], start=k4 == 0, stop=k4 == KD // 4 - 1)
                    mm.then_inc(sem("mod_part"), 1)

                def modulation_T(a):
                    pe.wait_ge(sem("modrow_moved"), b * ADA_ITEMS + a + 3)
                    pe.wait_ge(sem("mod_moved"), b * ADA_ITEMS + a + 1)
                    for c in range(2):
                        mm = pe.matmul(bank(7)[:, c * 96:c * 96 + 96], modrow[a % 2][:, c * P:(c + 1) * P], fold,
                                       start=True, stop=True)
                    mm.then_inc(sem("mod_sum"), 1)

                def hidden(s):
                    for moved in ("even_moved", "odd_moved"):
                        pe.wait_ge(sem(moved), b * (PAGES // 2) + PAGES // 2 + 1)
                    pe.wait_ge(sem("hid_ready"), b * 2 + s + 1)
                    for l in range(CMP):
                        mm = pe.matmul(bank(2 + s)[:, 0:P], w1[:, (s * CMP + l) * HD:(s * CMP + l + 1) * HD],
                                       XT[s][:, l * P:(l + 1) * P], start=l == 0, stop=l == CMP - 1)
                    mm.then_inc(sem("hid_sum"), 1)

                modulation(0)
                modulation(1)
                modulation_T(0)
                hidden(0)
                modulation(2)
                modulation_T(1)
                hidden(1)
                modulation(3)
                modulation_T(2)
                pe.wait_ge(sem("cmp_moved"), b + 1)
                pe.wait_ge(sem("hid_ready"), b * 2 + 2 + 1)
                pe.matmul(bank(4)[:, 0:P], w2[:, 0:HD], hid[0], start=True, stop=True)
                pe.wait_ge(sem("hid_ready"), b * 2 + 2 + 2)
                for h in range(KVH):
                    mm = pe.matmul(bank(4)[0:NC, P + h * HD:P + (h + 1) * HD], hid[1][:, h * NC:(h + 1) * NC], w2[:, HD:2 * HD],
                                   start=True, stop=True)
                mm.then_inc(sem("cmp_sum"), 1)
                modulation(4)
                modulation_T(3)
                modulation(5)
                modulation_T(4)
                modulation_T(5)

        def dve_setup(dve):
            dve.wait_ge(sem("params_T"), 1)
            dve.tensor_copy(params[:, 0:96], bank(6)[:, 0:96]).then_inc(sem("params_moved"), 1)
            dve.tensor_copy(params[:, P:P + 96], bank(6)[:, P:P + 96]).then_inc(sem("params_moved"), 1)
            dve.tensor_copy(params[:, 2 * P:2 * P + 115], bank(6)[:, 2 * P:2 * P + 115]).then_inc(sem("params_ready"), 1)
            n = 0
            for t, rows in enumerate((P, P, NB)):
                for k4 in range(KD // 4):
                    dve.wait_ge(sem("x_blocks"), n + 1)
                    dve.tensor_copy(xT3[:, 4 * k4:4 * k4 + 4, t * P:t * P + rows],
                                    bank(n % 2).rearrange("p (k c) -> p k c", k=4)[:, :, 0:rows]).then_inc(sem("x_moved"), 1)
                    n += 1
            dve.wait_ge(sem("x_moved"), 12)
            dve.sem_inc(sem("x_T"), 2)
            dve.wait_ge(sem("consts"), 4)

            c = sem("level_steps")
            bits = work[:, 1408:1536].bitcast(I32)
            dve.wait_ge(sem("row_xor"), 2)
            step(dve, c, dve.tensor_tensor(bits, bits, levels[:, 0:P].bitcast(I32), ALU.bitwise_xor))
            for l in range(6, -1, -1):
                lv = levels[:, l * P:(l + 1) * P]
                step(dve, c, dve.tensor_scalar(lv.bitcast(I32), bits, l, None, ALU.logical_shift_right))
                step(dve, c, dve.tensor_scalar(lv, lv.bitcast(I32), 1, None, ALU.is_equal))
                step(dve, c, dve.tensor_tensor(lv, lv, above[:], ALU.mult))

        def dve_compress(dve):
            dve.wait_ge(sem("hid_bias_sum"), 1)
            dve.wait_ge(sem("params_ready"), 1)
            dve.tensor_tensor(hid_bias, bank(3)[:, 0:2], cb1T, ALU.add).then_inc(sem("hid_bias_ready"), 1)
            dve.sem_inc(sem("even_moved"), 1)
            dve.sem_inc(sem("odd_moved"), 1)
            dve.sem_inc(sem("mod_moved"), 1)
            dve.sem_inc(sem("modrow_moved"), 2)
            dve.sem_inc(sem("hid_ready"), 2)
            dve.sem_inc(sem("cmp_moved"), 1)
            with dve.Fori(0, NB) as b:
                for pp in range(0, PAGES, 2):
                    dve.wait_ge(sem("page_T"), b * PAGES + pp + 1)
                    if pp == 0:
                        dve.wait_ge(sem("hid_sum"), b * 2 + 2)
                    for s in range(2):
                        mv = dve.tensor_copy(XT[s].rearrange("p (l h n) -> p h n l", h=KVH, n=NC)[:, :, 4 * pp:4 * pp + 4, :],
                                             bank(0)[:, 256 * s:256 * s + 256].rearrange("p (h n l) -> p h n l", h=KVH, n=4))
                    mv.then_inc(sem("even_moved"), 1)

                def modulation(a):
                    dve.wait_ge(sem("mod_part"), b * ADA_ITEMS + ADA_ITEMS + a + 1)
                    dve.wait_ge(sem("mod_sum"), b * ADA_ITEMS + a + 1)
                    dve.tensor_copy(modrow[a % 2], bank(5 + a % 2)[:, 0:256]).then_inc(sem("modrow_moved"), 1)

                def modulation_T(a):
                    dve.wait_ge(sem("mod_sum"), b * ADA_ITEMS + a + 3)
                    dve.tensor_scalar(modT[:, bass.ds(b * (ADA_ITEMS * 18) + a * 18, 18)].rearrange("p (c r) -> p c r", c=2),
                                      bank(7)[:, 0:192].rearrange("p (c r) -> p c r", c=2)[:, :, 0:9],
                                      1.0, None, ALU.mult).then_inc(sem("mod_moved"), 1)

                modulation(0)
                for a in range(1, 4):
                    modulation(a)
                    modulation_T(a - 1)
                dve.wait_ge(sem("cmp_sum"), b + 2)
                dve.tensor_scalar(ckT[:, bass.ds(b * P, P)], bank(4)[:, 0:P], 1.0, None, ALU.mult).then_inc(sem("ck_moved"), 1)
                dve.tensor_scalar(cvR[:, bass.ds(b * 2 * HD, 2 * HD)], bank(4)[0:NC, P:P + 2 * HD], 1.0, None,
                                  ALU.mult).then_inc(sem("cmp_moved"), 1)
                for a in range(4, 6):
                    modulation(a)
                    modulation_T(a - 1)
                modulation_T(5)


        full_base = [NB * 144, NB * 144, NB * 32, NB * 32]
        scl = work[:, 0:144]
        rstd = work[:, 144:144 + TC]
        wsm = work[:, 512:512 + KD * 40]
        gfm = work[0:40, 1152:1152 + TC]
        scl3 = v3(scl, 0, KD, 9)
        sq3 = hT3

        def act_norm(act, n, fm_ready):
            fm_ready(act)
            for q in range(4):
                act.activation(sq3[:, 4 * q:4 * q + 4, :], xT3[:, 4 * q:4 * q + 4, :], ACT.Square).then_inc(sem("squares"), 1)
            act.wait_ge(sem("square_sum"), n)
            act.activation(rstd, bank(0)[:, 0:TC], ACT.Sqrt, bias=eps_col, scale=1.0 / D).then_inc(sem("root"), 1)

        def pe_norm(pe, n):
            for q in range(4):
                pe.wait_ge(sem("squares"), 4 * (n - 1) + q + 1)
                for k in range(4 * q, 4 * q + 4):
                    mm = pe.matmul(bank(0)[:, 0:TC], ones[:], sq3[:, k, :], start=k == 0, stop=k == KD - 1)
            mm.then_inc(sem("square_sum"), 1)

        def dve_norm(dve, n, normT, m_shift, m_scale):
            c = sem("norm_steps")
            step(dve, c, dve.scalar_tensor_tensor(scl3, mod3[:, m_scale:m_scale + KD, :], 1.0,
                                                  normT.unsqueeze(2).to_broadcast([P, KD, 9]), ALU.add, ALU.mult))
            dve.wait_ge(sem("root"), n)
            step(dve, c, dve.reciprocal(rstd, rstd))
            step(dve, c, dve.tensor_tensor(hT3, xT3, rstd.unsqueeze(1).to_broadcast([P, KD, TC]), ALU.mult))
            for k in range(KD):
                dve.tensor_scalar(hT3[:, k, 0:T], hT3[:, k, 0:T], scl3[:, k, 0:1], mod3[:, m_shift + k, 0:1], ALU.mult, ALU.add
                                  ).then_inc(sem("h_prompt"), 1)
            step(dve, c, dve.tensor_tensor(hT3[:, :, T:TC], hT3[:, :, T:TC], scl3[:, :, 1:9], ALU.mult))
            dve.tensor_tensor(hT3[:, :, T:TC], hT3[:, :, T:TC], mod3[:, m_shift:m_shift + KD, 1:9], ALU.add).then_inc(sem("h_sample"), 1)

        proj_blocks = [0]

        def pe_wait_proj_rows(pe, n):
            pe.wait_ge(sem("h_sample"), n)
            pe.wait_ge(sem("h_prompt"), KD * n)

        def item_src(w, first):
            return w.rearrange("(k p) n -> p k n", p=P)[:, :, bass.ds(first, 256)]

        def sp_project(sp, G0, n0, items, w, col0):
            def load(j, n, first):
                sp.wait_ge(sem("proj_sum"), n + 2)
                sp.dma_start(ring[:, j, :].rearrange("p (k n) -> p k n", k=KD), item_src(w, first)).then_inc(full[j], 16)
            rounds = items // RING
            with sp.Fori(0, rounds) as i:
                for j in range(RING):
                    load((G0 + j) % RING, i * 8 + (n0 + 2 * j), i * 1024 + (col0 + 256 * j))
            for m in range(rounds * RING, items):
                load((G0 + m) % RING, n0 + 2 * m, col0 + 256 * m)

        def pe_project(pe, G0, n0, items, rhs3, base=full_base):
            def item(G_slot, full_n, n):
                pe.wait_ge(full[G_slot], full_n)
                for c in range(2):
                    bk = bank(c)
                    pe.wait_ge(sem("proj_moved"), n + (c + 1))
                    for k in range(KD):
                        mm = pe.matmul(bk[:, 0:TC], ring[:, G_slot, k * 256 + c * P:k * 256 + (c + 1) * P], rhs3[:, k, :],
                                       start=k == 0, stop=k == KD - 1)
                    mm.then_inc(sem("proj_sum"), 1)
            rounds = items // RING
            with pe.Fori(0, rounds) as i:
                for j in range(RING):
                    G = G0 + j
                    item(G % RING, i * 16 + (base[G % RING] + 16 * (G // RING + 1)), i * 8 + (n0 + 2 * j))
            for m in range(rounds * RING, items):
                G = G0 + m
                item(G % RING, base[G % RING] + 16 * (G // RING + 1), n0 + 2 * m)

        def dve_project(dve, n0, items, dst, block0):
            def move(c, n, at_):
                dve.wait_ge(sem("proj_sum"), n + (8 + c + 1))
                dve.tensor_scalar(dst[:, bass.ds(at_, TC)], bank(c)[:, 0:TC], 1.0, None, ALU.mult).then_inc(sem("proj_moved"), 1)
            rounds = items // RING
            with dve.Fori(0, rounds) as i:
                for j in range(RING):
                    for c in range(2):
                        move(c, i * 8 + (n0 + 2 * j), i * (8 * TC) + (block0 + 2 * j + c) * TC)
            for m in range(rounds * RING, items):
                for c in range(2):
                    move(c, n0 + 2 * m, (block0 + 2 * m + c) * TC)

        w_in = io["w_in"][0]
        G_IN, G_QKV = 0, 16
        G_NEXT = 26

        def sp_in(sp):
            sp.wait_ge(sem("mod_part"), ADA_ITEMS + NB * ADA_ITEMS)
            sp.wait_ge(sem("cmp_sum"), NB + 1)
            wk = w_in.rearrange("(k p) n -> p k n", p=P)
            w3 = v3(wsm, 0, KD, 40)
            sp.wait_ge(sem("mod_sum"), 2 + NB * ADA_ITEMS)
            sp.dma_start(w3[:, :, 0:24], wk[:, :, COL_GATES:COL_GATES + 24]).then_inc(sem("wsm_in"), 16)
            sp.dma_start(w3[:, :, 24:40], wk[:, :, COL_BA:COL_BA + 16]).then_inc(sem("wsm_in"), 16)
            sp_project(sp, G_IN, 0, 16, w_in, COL_G)
            sp_project(sp, G_QKV, 32, 10, w_in, 0)

        def act_in(act):
            act_norm(act, 1, lambda a: a.wait_ge(sem("cmp_sum"), NB + 1))
            act.wait_ge(sem("gates_fm"), 1)
            act.activation(gfm, bank(2)[0:40, 0:TC], ACT.Copy).then_inc(sem("gates_fm_moved"), 1)
            act.wait_ge(sem("gates_T"), 1)
            act.wait_ge(sem("consts"), 12)
            act.activation(v3(gt, 0, 3, 40)[:, 0:2, :], v3(bank(3), 0, 3, 40)[:, 0:2, :], ACT.Copy).then_inc(sem("gates_moved"), 1)
            act.activation(gt[0:NB, 80:120], bank(3)[0:NB, 80:120], ACT.Copy).then_inc(sem("gates_moved"), 1)

        def pe_in(pe):
            pe_norm(pe, 1)
            pe.sem_inc(sem("proj_sum"), 8)
            pe_wait_proj_rows(pe, 1)
            pe.wait_ge(sem("wsm_in"), 32)
            for k in range(KD):
                mm = pe.matmul(bank(2)[0:40, 0:TC], wsm[:, k * 40:(k + 1) * 40], hT3[:, k, :], start=k == 0, stop=k == KD - 1)
            mm.then_inc(sem("gates_fm"), 1)
            pe_project(pe, G_IN, 0, 16, hT3)
            pe.wait_ge(sem("gates_fm_moved"), 1)
            for t, n in enumerate((P, P, NB)):
                mm = pe.transpose(bank(3)[0:n, t * 40:(t + 1) * 40], gfm[:, t * P:t * P + n], ident[0:40, 0:40])
            mm.then_inc(sem("gates_T"), 1)
            pe_conv(pe)
            pe_project(pe, G_QKV, 32, 10, hT3)

        def dve_in(dve):
            c = sem("norm_steps")
            dve.wait_ge(sem("mod_moved"), 1 + NB * ADA_ITEMS)
            step(dve, c, dve.tensor_tensor(mod3, mod3, bias_ada.unsqueeze(2).to_broadcast([P, 96, 9]), ALU.add))
            dve.sem_inc(sem("proj_moved"), 2)
            dve_norm(dve, 1, norm1T, M_SH1, M_SC1)
            dve_project(dve, 0, 16, pT, B_GQ)


        crows = work[0:11, 0:3072]
        srows = work[0:24, 3072:6144]
        stT = v3(work, 6144, 24, 24)
        csum = v3(work, 6720, 24, NB)
        cmul = v3(work, 6912, 24, NB)
        ctmp = [work[:, 3072 + 256 * i:3328 + 256 * i] for i in range(4)]
        qkv3 = pT3[:, B_GQ:B_Z, :]
        cw = lambda i: conv_wT[:, 24 * i:24 * i + 24]
        mix3 = hT3

        decay_in = cols("decay_in", 16)
        beta = cols("beta", 24)
        gl = cols("gl", 24)
        gates = cols("gates", 72)
        spa = cols("spa", 24)
        spb = cols("spb", 24)
        eG = cols("eG", 16)
        eGl = cols("eGl", 16)
        eGd = cols("eGd", 16)
        gt3, beta3, gl3 = v3(gt, 0, 3, 40), v3(beta, 0, 3, 8), v3(gl, 0, 3, 8)
        B2 = lambda ap, n: ap.unsqueeze(2).to_broadcast([ap.shape[0], ap.shape[1], n])
        B1 = lambda ap, n: ap.unsqueeze(1).to_broadcast([ap.shape[0], n, ap.shape[1]])

        R = [v3(work, 1024 * i, HEADS, P) for i in range(7)]
        KR, VR, SG, AM, QK, PM, QM = R
        SS, YV = v3(hT, 0, HEADS, P), v3(hT, 1024, HEADS, P)

        def sp_delta(sp):
            sp.wait_ge(sem("proj_sum"), 8 + 52)
            for i in range(2):
                j = (G_NEXT + i) % RING
                sp.dma_start(ring[:, j, :].rearrange("p (a e) -> p a e", e=HD),
                             io["state_gdn"][0, 4 * i:4 * i + 4].rearrange("b h d e -> d (b h) e")).then_inc(full[j], 16)

        def act_early(act):
            act.wait_ge(sem("x_moved"), 12)
            act.wait_ge(sem("mod_part"), 7)
            act.dma_start(srows, io["state_conv"][0].rearrange("b i c -> (b i) c")).then_inc(sem("state_in"), 16)
            act.dma_start(decay_in[:, 0:8], io["gdn_a_log"].to_broadcast([P, 8])).then_inc(sem("decay_in"), 16)
            act.dma_start(decay_in[:, 8:16], io["gdn_dt_bias"].to_broadcast([P, 8])).then_inc(sem("decay_in"), 16)

        def pe_conv(pe):
            pe.wait_ge(sem("proj_moved"), 2 + 32)
            pe.wait_ge(sem("gates_moved"), 2)
            for c in range(24):
                if c % 4 == 0 and c >= 16:
                    pe.wait_ge(sem("crows_moved"), c // 4 - 3)
                mm = pe.transpose(bank(2 + (c // 4) % 4)[0:11, (c % 4) * P:(c % 4 + 1) * P], qkv3[:, c, 253:264], ident[:])
                if c % 4 == 3:
                    mm.then_inc(sem("crows_T"), 1)
            pe.wait_ge(sem("state_in"), 16)
            for c in range(24):
                mm = pe.transpose(bank(6 + c // 12)[:, (c % 12) * 24:(c % 12 + 1) * 24], srows[:, c * P:(c + 1) * P], ident[0:24, 0:24])
            mm.then_inc(sem("state_T"), 1)

        def dve_conv(dve):
            c = sem("conv_steps")
            dve.wait_ge(sem("gates_T"), 1)
            for q in range(6):
                dve.wait_ge(sem("crows_T"), q + 1)
                dve.tensor_copy(crows[:, 512 * q:512 * q + 512], bank(2 + q % 4)[0:11, :]).then_inc(sem("crows_moved"), 1)
            dve.wait_ge(sem("state_T"), 1)
            for q in range(2):
                step(dve, c, dve.tensor_copy(stT[:, 12 * q:12 * q + 12, :], v3(bank(6 + q), 0, 12, 24)))
            st4 = stT.rearrange("p c (b i) -> p c b i", i=3)
            step(dve, c, dve.tensor_tensor(csum, qkv3[:, :, T:TC], B2(cw(3), NB), ALU.mult))
            for i in range(3):
                step(dve, c, dve.tensor_tensor(cmul, st4[:, :, :, i], B2(cw(i), NB), ALU.mult))
                step(dve, c, dve.tensor_tensor(csum, csum, cmul, ALU.add))
            mark(sem("csum_ready"), dve.tensor_copy(stT[:, 0, 0:1], csum[:, 0, 0:1]))
            for b in range(24):
                t = ctmp[b % 4]
                if b >= 4:
                    dve.wait_ge(sem("conv_silu"), b - 3)
                x = qkv3[:, b, 0:T]
                w = lambda i: cw(i)[:, b:b + 1]
                step(dve, c, dve.tensor_scalar(t, x, w(3), None, ALU.mult))
                step(dve, c, dve.scalar_tensor_tensor(t[:, 1:T], x[:, 0:T - 1], w(2), t[:, 1:T], ALU.mult, ALU.add))
                step(dve, c, dve.scalar_tensor_tensor(t[:, 2:T], x[:, 0:T - 2], w(1), t[:, 2:T], ALU.mult, ALU.add))
                dve.scalar_tensor_tensor(t[:, 3:T], x[:, 0:T - 3], w(0), t[:, 3:T], ALU.mult, ALU.add).then_inc(sem("conv_sum"), 1)

        def act_conv(act):
            silu = [0]

            def conv_silu():
                b = silu[0]
                if b < 24:
                    act.wait_ge(sem("conv_sum"), b + 1)
                    act.activation(qkv3[:, b, 0:T], ctmp[b % 4], ACT.Silu).then_inc(sem("conv_silu"), 1)
                    silu[0] += 1

            for n in range(20):
                act.wait_ge(sem("proj_sum"), 8 + 32 + n + 1)
                act.activation(pT3[:, n, :], bank(n % 2)[:, 0:TC], ACT.Copy).then_inc(sem("proj_moved"), 1)
                if n == 3:
                    act.wait_ge(sem("csum_ready"), 1)
                    act.activation(qkv3[:, :, T:TC], csum, ACT.Silu).then_inc(sem("csilu"), 1)
                if n >= 4:
                    conv_silu()
                    conv_silu()
            for _ in range(24):
                conv_silu()
            act.activation(pT3[:, B_Z:NBLK, :], pT3[:, B_Z:NBLK, :], ACT.Silu).then_inc(sem("z_ready"), 1)

        def act_delta_gates(act):
            act.wait_ge(sem("conv_silu"), 24)
            act.wait_ge(sem("csilu"), 1)
            act.wait_ge(sem("proj_sum"), 8 + 52)
            for q in range(4):
                act.activation(hT3[:, 4 * q:4 * q + 4, :], qkv3[:, 4 * q:4 * q + 4, :], ACT.Square).then_inc(sem("qk_squares"), 1)
            for b in range(16):
                act.wait_ge(sem("qk_sums"), b + 1)
                act.activation(hT3[:, b, :], bank(b % 4)[:, 0:TC], ACT.Sqrt, bias=eps_col).then_inc(sem("qk_root"), 1)
            act.activation(beta3, gt3[:, :, 24:32], ACT.Sigmoid).then_inc(sem("beta_ready"), 1)
            act.activation(v3(gates, 0, 3, 24), gt3[:, :, 0:24], ACT.Sigmoid).then_inc(sem("gates_ready"), 1)
            act.wait_ge(sem("sp_abs"), 1)
            act.activation(spb, spb, ACT.Exp, scale=-1.0).then_inc(sem("act_steps"), 1)
            act.activation(decay_in[:, 0:8], decay_in[:, 0:8], ACT.Exp).then_inc(sem("act_steps"), 1)
            act.wait_ge(sem("act_steps"), 2)
            act.activation(spb, spb, ACT.Ln, bias=ones[:, 0:1]).then_inc(sem("softplus"), 1)

        def pe_delta_norm(pe):
            for b in range(16):
                if b % 4 == 0:
                    pe.wait_ge(sem("qk_squares"), b // 4 + 1)
                if b >= 4:
                    pe.wait_ge(sem("qk_root"), b - 3)
                pe.matmul(bank(b % 4)[:, 0:TC], ones[:], hT3[:, b, :], start=True, stop=True).then_inc(sem("qk_sums"), 1)

        def dve_delta_gates(dve):
            c = sem("gate_steps")
            dve.wait_ge(sem("decay_in"), 32)
            dve.wait_ge(sem("gates_moved"), 2)
            spa3, spb3 = v3(spa, 0, 3, 8), v3(spb, 0, 3, 8)
            step(dve, c, dve.tensor_tensor(spa3, gt3[:, :, 32:40], B1(decay_in[:, 8:16], 3), ALU.add))
            step(dve, c, dve.tensor_scalar(spb, spa, -1.0, None, ALU.mult))
            dve.tensor_tensor(spb, spb, spa, ALU.max).then_inc(sem("sp_abs"), 1)
            for b in range(16):
                dve.wait_ge(sem("qk_root"), b + 1)
                step(dve, c, dve.reciprocal(hT3[:, b, :], hT3[:, b, :]))
                if b < 8:
                    dve.scalar_tensor_tensor(qkv3[:, b, :], qkv3[:, b, :], SCALE, hT3[:, b, :], ALU.mult, ALU.mult).then_inc(sem("qk_ready"), 1)
                else:
                    dve.tensor_tensor(qkv3[:, b, :], qkv3[:, b, :], hT3[:, b, :], ALU.mult).then_inc(sem("qk_ready"), 1)
            dve.wait_ge(sem("softplus"), 1)
            step(dve, c, dve.scalar_tensor_tensor(spa, spa, 0.0, spb, ALU.max, ALU.add))
            dve.scalar_tensor_tensor(gl3, spa3, -1.0, B1(decay_in[:, 0:8], 3), ALU.mult, ALU.mult).then_inc(sem("log_decay"), 1)
            dve.wait_ge(sem("log_decay"), 1)
            dve.wait_ge(sem("decay_sums"), 1)
            step(dve, c, dve.tensor_copy(spa[:, 0:16], bank(4)[:, 16:32]))
            dve.tensor_tensor(eGd, spa[:, 0:16], bank(4)[:, 0:16], ALU.subtract).then_inc(sem("decay_left"), 1)

        def pe_delta_gates(pe):
            pe.wait_ge(sem("log_decay"), 1)
            pe.matmul(bank(4)[:, 0:16], upto[:], gl[:, 0:16], start=True, stop=True)
            pe.matmul(bank(4)[:, 16:32], ones[:], gl[:, 0:16], start=True, stop=True).then_inc(sem("decay_sums"), 1)

        def act_decay(act):
            act.wait_ge(sem("decay_left"), 1)
            act.activation(eG, bank(4)[:, 0:16], ACT.Exp).then_inc(sem("decay_exps"), 1)
            act.activation(eGl, bank(4)[:, 16:32], ACT.Exp).then_inc(sem("decay_exps"), 1)
            act.activation(eGd, eGd, ACT.Exp).then_inc(sem("decay_exps"), 1)

        col = lambda j: slice(j * P, (j + 1) * P)
        HALF = lambda u: slice(4 * u, 4 * u + 4)
        pair = lambda i: ps[:, i:i + 2, :].rearrange("p a (b c) -> p (a b) c", c=P)
        hb = lambda i, h: ps[:, i + h // 4, (h % 4) * P:(h % 4 + 1) * P]

        def pe_chunk(pe, j):
            n = lambda per, k=0: per * j + k
            pe.wait_ge(sem("sg_ready"), n(1, 1))
            if j:
                pe.wait_ge(sem("state_new"), 1)
                pe.wait_ge(sem("delta_out"), 1)
            for u in range(2):
                mm = pe.matmul(bank(u), upto[:], SG[:, HALF(u), :], start=True, stop=True)
            mm.then_inc(sem("decay_mm"), 1)
            for h in range(HEADS):
                mm = pe.matmul(hb(2, h), SG[:, h, :], upto[:], start=True, stop=True)
            mm.then_inc(sem("decay_mm"), 1)
            if j == 0:
                pe.wait_ge(sem("decay_exps"), 2)
            for h in range(HEADS):
                mm = pe.matmul(hb(4, h), gl3[:, j, h:h + 1].to_broadcast([P, P]), upto[:], start=True, stop=True)
            mm.then_inc(sem("decay_mm"), 1)
            pe.wait_ge(sem("qk_ready"), 16)
            for h in range(HEADS):
                kT = qkv3[:, 8 + h, col(j)]
                mm = pe.matmul(hb(6, h), kT, kT, start=True, stop=True)
            mm.then_inc(sem("kk_mm"), 1)
            pe.wait_ge(sem("decay_moved"), n(3, 1))
            for h in range(HEADS):
                mm = pe.matmul(hb(0, h), qkv3[:, 8 + h, col(j)], qkv3[:, h, col(j)], start=True, stop=True)
            mm.then_inc(sem("qk_mm"), 1)
            pe.wait_ge(sem("decay_moved"), n(3, 2))
            for h in range(HEADS):
                mm = pe.transpose(hb(2, h), qkv3[:, 8 + h, col(j)], ident[:])
            mm.then_inc(sem("rows_T"), 1)
            pe.wait_ge(sem("decay_moved"), n(3, 3))
            for h in range(HEADS):
                mm = pe.transpose(hb(4, h), qkv3[:, 16 + h, col(j)], ident[:])
            mm.then_inc(sem("rows_T"), 1)
            pe.wait_ge(sem("q0_ready"), n(1, 1))
            pe.wait_ge(sem("am_ready"), n(1, 1))
            for h in range(HEADS):
                mm = pe.transpose(hb(6, h), QM[:, h, :], ident[:])
            mm.then_inc(sem("p0_T"), 1)
            for l in range(1, 7):
                for u in range(2):
                    i = 2 * (6 * j + l - 1) + u
                    pe.wait_ge(sem("level_ready"), i + 1)
                    if l == 1:
                        pe.wait_ge(sem("p0_ready"), n(1, 1))
                        pe.wait_ge(sem("qk_masked"), n(1, 1))
                    else:
                        pe.wait_ge(sem("p_new"), i - 1)
                    for h in range(4 * u, 4 * u + 4):
                        mm = pe.matmul(hb(0, h), SG[:, h, :], PM[:, h, :], start=True, stop=True)
                    mm.then_inc(sem("y_mm"), 1)
                for u in range(2):
                    i = 2 * (6 * j + l - 1) + u
                    pe.wait_ge(sem("y_moved"), i + 1)
                    if l == 1:
                        pe.wait_ge(sem("rows_moved"), n(2, 2))
                    else:
                        pe.wait_ge(sem("q_new"), 2 * (5 * j + l - 2) + u + 1)
                    for h in range(4 * u, 4 * u + 4):
                        mm = pe.matmul(hb(2, h), QM[:, h, :], YV[:, h, :], start=True, stop=True)
                    mm.then_inc(sem("py_mm"), 1)
                    if l < 6:
                        for h in range(4 * u, 4 * u + 4):
                            mm = pe.matmul(hb(4, h), YV[:, h, :], QM[:, h, :], start=True, stop=True)
                        mm.then_inc(sem("yq_mm"), 1)
            pe.wait_ge(sem("p_new"), 12 * (j + 1))
            if j:
                for h in range(HEADS):
                    mm = pe.matmul(hb(2, h), qkv3[:, 8 + h, col(j)], SS[:, h, :], start=True, stop=True)
                mm.then_inc(sem("ks_mm"), 1)
            pe.wait_ge(sem("r_ready"), n(1, 1))
            for h in range(HEADS):
                mm = pe.matmul(hb(6, h), PM[:, h, :], VR[:, h, :], start=True, stop=True)
            mm.then_inc(sem("vn_mm"), 1)
            pe.wait_ge(sem("vn_moved"), n(1, 1))
            pe.wait_ge(sem("qg_ready"), n(1, 1))
            for h in range(HEADS):
                if j:
                    pe.matmul(hb(0, h), SS[:, h, :], qkv3[:, h, col(j)], start=True, stop=False)
                mm = pe.matmul(hb(0, h), YV[:, h, :], QK[:, h, :], start=not j, stop=True)
            mm.then_inc(sem("o_mm"), 1)
            pe.wait_ge(sem("kd_ready"), n(1, 1))
            for h in range(HEADS):
                mm = pe.matmul(hb(4, h), KR[:, h, :], YV[:, h, :], start=True, stop=True)
            mm.then_inc(sem("s_mm"), 1)

        def act_chunk(act, j):
            n = lambda per, k=0: per * j + k
            if j:
                act.wait_ge(sem("vn_used"), 1)
            for i, dst in enumerate((AM, QK, YV)):
                act.wait_ge(sem("decay_mm"), n(3, i + 1))
                if i == 2:
                    act.wait_ge(sem("qk_ready"), 16)
                act.activation(dst, pair(2 * i), ACT.Exp).then_inc(sem("decay_moved"), 1)
            for i, dst in enumerate((KR, VR)):
                act.wait_ge(sem("rows_T"), n(2, i + 1))
                act.activation(dst, pair(2 + 2 * i), ACT.Copy).then_inc(sem("rows_moved"), 1)
            act.wait_ge(sem("p0_T"), n(1, 1))
            act.activation(PM, pair(6), ACT.Copy).then_inc(sem("p0_ready"), 1)
            act.wait_ge(sem("q_scaled"), n(1, 1))
            for l in range(1, 7):
                for u in range(2):
                    i = 2 * (6 * j + l - 1) + u
                    act.wait_ge(sem("y_mm"), i + 1)
                    if l > 1:
                        act.wait_ge(sem("yq_mm"), 2 * (5 * j + l - 2) + u + 1)
                    act.activation(YV[:, HALF(u), :], v3(bank(u), 0, 4, P), ACT.Copy).then_inc(sem("y_moved"), 1)
            act.wait_ge(sem("vn_mm"), n(1, 1))
            act.wait_ge(sem("py_mm"), 12 * (j + 1))
            act.activation(YV, pair(6), ACT.Copy).then_inc(sem("vn_moved"), 1)

        def dve_chunk(dve, j):
            n = lambda per, k=0: per * j + k
            c = sem("chunk_steps")
            if j == 0:
                dve.wait_ge(sem("crows_out"), 32)
                dve.wait_ge(sem("conv_silu"), 24)
                dve.wait_ge(sem("csilu"), 1)
            dve.tensor_tensor(SG, B1(above[:], HEADS), B2(gl3[:, j, :], P), ALU.mult).then_inc(sem("sg_ready"), 1)
            dve.wait_ge(sem("decay_moved"), n(3, 1))
            step(dve, c, dve.tensor_tensor(AM, AM, B1(above[:], HEADS), ALU.mult))
            step(dve, c, dve.tensor_tensor(AM, AM, B2(beta3[:, j, :], P), ALU.mult))
            dve.wait_ge(sem("kk_mm"), n(1, 1))
            step(dve, c, dve.tensor_tensor(AM, AM, pair(6), ALU.mult))
            dve.wait_ge(sem("decay_mm"), n(3, 3))
            step(dve, c, dve.tensor_tensor(SG, AM, B1(levels[:, 0:P], HEADS), ALU.mult))
            dve.sem_inc(sem("am_ready"), 1)
            dve.tensor_tensor(QM, B1(ident[:], HEADS), SG, ALU.subtract).then_inc(sem("q0_ready"), 1)
            dve.wait_ge(sem("q0_ready"), n(1, 1))
            for u in range(2):
                dve.tensor_tensor(SG[:, HALF(u), :], AM[:, HALF(u), :], B1(levels[:, P:2 * P], 4), ALU.mult).then_inc(sem("level_ready"), 1)
            dve.wait_ge(sem("decay_moved"), n(3, 2))
            step(dve, c, dve.tensor_tensor(QK, QK, B1(upto[:], HEADS), ALU.mult))
            dve.wait_ge(sem("qk_mm"), n(1, 1))
            dve.tensor_tensor(QK, QK, pair(0), ALU.mult).then_inc(sem("qk_masked"), 1)
            dve.wait_ge(sem("decay_moved"), n(3, 3))
            dve.tensor_tensor(qkv3[:, 0:8, col(j)], qkv3[:, 0:8, col(j)], YV, ALU.mult).then_inc(sem("q_scaled"), 1)
            dve.wait_ge(sem("q_scaled"), n(1, 1))
            dve.sem_inc(sem("qg_ready"), 1)
            dve.wait_ge(sem("rows_moved"), n(2, 1))
            dve.wait_ge(sem("decay_exps"), 3)
            dve.tensor_tensor(KR, KR, B2(v3(eGd, 0, 2, 8)[:, j, :], P), ALU.mult).then_inc(sem("kd_ready"), 1)
            for l in range(1, 7):
                for u in range(2):
                    i = 2 * (6 * j + l - 1) + u
                    if l == 1:
                        dve.wait_ge(sem("p0_ready"), n(1, 1))
                    dve.wait_ge(sem("py_mm"), i + 1)
                    dve.tensor_tensor(PM[:, HALF(u), :], PM[:, HALF(u), :], v3(bank(2 + u), 0, 4, P), ALU.subtract).then_inc(sem("p_new"), 1)
                    if l < 6:
                        dve.tensor_tensor(SG[:, HALF(u), :], AM[:, HALF(u), :], B1(levels[:, (l + 1) * P:(l + 2) * P], 4), ALU.mult
                                          ).then_inc(sem("level_ready"), 1)
                        dve.wait_ge(sem("yq_mm"), 2 * (5 * j + l - 1) + u + 1)
                        dve.tensor_tensor(QM[:, HALF(u), :], QM[:, HALF(u), :], v3(bank(4 + u), 0, 4, P), ALU.subtract).then_inc(sem("q_new"), 1)
            dve.wait_ge(sem("rows_moved"), n(2, 2))
            if j:
                dve.wait_ge(sem("ks_mm"), 1)
                step(dve, c, dve.tensor_tensor(SG, pair(2), B2(v3(eG, 0, 2, 8)[:, j, :], P), ALU.mult))
                step(dve, c, dve.tensor_tensor(VR, VR, SG, ALU.subtract))
            dve.tensor_tensor(VR, VR, B2(beta3[:, j, :], P), ALU.mult).then_inc(sem("r_ready"), 1)
            if j:
                dve.wait_ge(sem("o_mm"), 2)
                step(dve, c, dve.tensor_tensor(SS, SS, B2(v3(eGl, 0, 2, 8)[:, j, :], P), ALU.mult))
            dve.wait_ge(sem("o_mm"), n(1, 1))
            dve.tensor_copy(mix3[:, 8:16, col(j)], pair(0)).then_inc(sem("delta_out"), 1)
            dve.wait_ge(sem("s_mm"), n(1, 1))
            dve.sem_inc(sem("vn_used"), 1)
            if j:
                dve.tensor_tensor(SS, SS, pair(4), ALU.add).then_inc(sem("state_new"), 1)
            else:
                dve.tensor_copy(SS, pair(4)).then_inc(sem("state_new"), 1)
            dve.wait_ge(sem("state_new"), j + 1)

        def pool_delta(pool):
            c = sem("level_consts")
            mi = levels[:, 0:P].bitcast(I32)
            pool.wait_ge(sem("consts"), 12)
            n = 0
            pool.wait_ge(sem("crows_moved"), 6)
            pool.dma_start(outs["conv_p"][0, 0], crows[0:3, :]).then_inc(sem("crows_out"), 16)
            pool.dma_start(outs["conv_s"][0, :, 2], crows[3:11, :]).then_inc(sem("crows_out"), 16)
            pool.dma_start(outs["conv_s"][0, :, 0:2], io["state_conv"][0, :, 1:3]).then_inc(sem("conv_copied"), 16)
            pool.wait_ge(sem("state_new"), 2)
            pool.dma_start(outs["gdn_p"][0, 0].rearrange("h d e -> d h e"), SS).then_inc(sem("state_out"), 16)
        out_sems.update(crows_out=32, conv_copied=16, state_out=16)


        W = lambda a, n: work[:, a:a + n]
        kq2 = W(0, 128)
        kq3 = v3(work, 0, 64, 2)
        vcol, prod, egb, betab = W(128, 64), W(192, 64), W(256, 64), W(320, 64)
        gdiag = work[0:8, 384:512]
        dt1, vn, dt2 = W(576, 64), W(640, 64), W(704, 64)
        krow, vrow = work[0:64, 768:896], work[0:64, 896:1024]
        vdiag = [v3(work, 1024, 4, P)[0:64], v3(work, 1536, 4, P)[0:64]]
        osq, oroot = v3(work, 2048, HEADS, TC), v3(work, 4160, HEADS, TC)
        bh = lambda ap: ap.rearrange("p (b h) -> p h b", h=HEADS)
        state_slot = [(G_NEXT + i) % RING for i in range(2)]

        def dve_step(dve):
            c = sem("step_steps")
            dve.wait_ge(sem("s_mm"), 2)
            for i, blk in enumerate((B_GK, B_GQ)):
                step(dve, c, dve.tensor_copy(bh(kq2.rearrange("p (a t) -> p a t", t=2)[:, :, i]), pT3[:, blk:blk + 8, T:TC]))
            step(dve, c, dve.tensor_copy(bh(vcol), pT3[:, B_GV:B_GV + 8, T:TC]))
            m8 = ident[0:8, 0:8].unsqueeze(2).to_broadcast([8, 8, 8])
            g8 = gdiag.rearrange("p (t b h) -> p t b h", t=2, b=8)
            step(dve, c, dve.tensor_tensor(g8[:, 0], m8, B1(gl3[0:8, 2, :], 8), ALU.mult))
            step(dve, c, dve.tensor_tensor(g8[:, 1], m8, B1(beta3[0:8, 2, :], 8), ALU.mult))
            dve.tensor_tensor(prod, kq3[:, :, 0], kq3[:, :, 1], ALU.mult).then_inc(sem("step_ready"), 1)
            dve.wait_ge(sem("step_ks"), 1)
            dve.wait_ge(sem("egb_ready"), 2)
            ks = v3(bank(2), 0, 64, 2)
            step(dve, c, dve.tensor_tensor(dt1, ks[:, :, 0], egb, ALU.mult))
            step(dve, c, dve.tensor_tensor(vn, vcol, dt1, ALU.subtract))
            dve.tensor_tensor(vn, vn, betab, ALU.mult).then_inc(sem("vn_ready"), 1)
            dve.wait_ge(sem("vn_ready"), 1)
            step(dve, c, dve.tensor_tensor(dt1, vn, bank(1)[:, 0:64], ALU.mult))
            step(dve, c, dve.tensor_tensor(dt2, ks[:, :, 1], egb, ALU.mult))
            dve.tensor_tensor(mix3[:, 8:16, T:TC], bh(dt1), bh(dt2), ALU.add).then_inc(sem("delta_out"), 1)
            dve.wait_ge(sem("step_rows"), 1)
            step(dve, c, dve.tensor_copy(krow, bank(3)[0:64, 0:128]))
            dve.tensor_copy(vrow, bank(3)[0:64, 128:256]).then_inc(sem("step_rows_moved"), 1)
            dve.wait_ge(sem("step_rows_moved"), 1)
            for q in range(17):
                if q < 16:
                    if q >= 2:
                        dve.wait_ge(sem("outer"), q - 1)
                    dve.tensor_tensor(vdiag[q % 2], vrow.unsqueeze(1).to_broadcast([64, 4, P]),
                                      B2(ident[0:64, 4 * q:4 * q + 4], P), ALU.mult).then_inc(sem("vdiag_ready"), 1)
                if q >= 1:
                    g = q - 1
                    dve.wait_ge(sem("decayed"), g // 8 + 1)
                    dve.wait_ge(sem("outer"), g + 1)
                    s = ring[:, state_slot[g // 8], (g % 8) * 512:(g % 8 + 1) * 512]
                    dve.tensor_tensor(s, s, bank(4 + g % 4), ALU.add).then_inc(sem("outer_added"), 1)
            for q in range(4):
                dve.wait_ge(sem("o_root"), 2 * q + 2)
                step(dve, c, dve.reciprocal(oroot[:, 2 * q:2 * q + 2, :], oroot[:, 2 * q:2 * q + 2, :]))
            o8 = mix3[:, 8:16, :]
            step(dve, c, dve.tensor_tensor(o8, o8, oroot, ALU.mult))
            dve.wait_ge(sem("z_ready"), 1)
            dve.scalar_tensor_tensor(o8, o8, gnT, pT3[:, B_Z:NBLK, :], ALU.mult, ALU.mult).then_inc(sem("delta_mixed"), 1)

        def pe_step(pe):
            pe.wait_ge(sem("step_ready"), 1)
            pe.wait_ge(sem("state_new"), 2)
            pe.wait_ge(sem("delta_out"), 2)
            pe.matmul(bank(0)[:, 0:128], ones[0:8, :], gdiag, start=True, stop=True).then_inc(sem("step_bc"), 1)
            pe.matmul(bank(1)[:, 0:64], ones[:], prod, start=True, stop=True)
            for p in range(64):
                if p % 32 == 0:
                    pe.wait_ge(full[state_slot[p // 32]], full_base[state_slot[p // 32]] + 16 * ((G_NEXT + p // 32) // RING + 1))
                mm = pe.matmul(bank(2)[:, 2 * p:2 * p + 2], ring[:, state_slot[p // 32], (p % 32) * P:(p % 32 + 1) * P],
                               kq2[:, 2 * p:2 * p + 2], start=True, stop=True)
            mm.then_inc(sem("step_ks"), 1)
            pe.wait_ge(sem("vn_ready"), 1)
            pe.transpose(bank(3)[0:64, 0:128], kq3[:, :, 0], ident[:])
            pe.transpose(bank(3)[0:64, 128:256], vn, ident[:]).then_inc(sem("step_rows"), 1)
            pe.wait_ge(sem("step_rows_moved"), 1)
            for g in range(16):
                pe.wait_ge(sem("vdiag_ready"), g + 1)
                if g >= 4:
                    pe.wait_ge(sem("outer_added"), g - 3)
                pe.matmul(bank(4 + g % 4), krow, vdiag[g % 2], start=True, stop=True).then_inc(sem("outer"), 1)
            for h in range(HEADS):
                pe.wait_ge(sem("o_squares"), 1)
                if h >= 4:
                    pe.wait_ge(sem("o_root"), h - 3)
                pe.matmul(bank(h % 4)[:, 0:TC], ones[:], osq[:, h, :], start=True, stop=True).then_inc(sem("o_sums"), 1)

        def act_step(act):
            act.wait_ge(sem("step_bc"), 1)
            act.activation(egb, bank(0)[:, 0:64], ACT.Exp).then_inc(sem("egb_ready"), 1)
            act.activation(betab, bank(0)[:, 64:128], ACT.Copy).then_inc(sem("egb_ready"), 1)
            act.wait_ge(sem("delta_out"), 3)
            act.activation(osq, mix3[:, 8:16, :], ACT.Square).then_inc(sem("o_squares"), 1)
            for h in range(HEADS):
                act.wait_ge(sem("o_sums"), h + 1)
                act.activation(oroot[:, h, :], bank(h % 4)[:, 0:TC], ACT.Sqrt, bias=eps_col, scale=1.0 / HD).then_inc(sem("o_root"), 1)

        def pool_step(pool):
            pool.wait_ge(sem("step_ks"), 1)
            pool.wait_ge(sem("egb_ready"), 1)
            for i in range(2):
                s = ring[:, state_slot[i], :].rearrange("p (a e) -> p a e", e=HD)
                pool.tensor_tensor(s, s, B2(egb[:, 32 * i:32 * i + 32], HD), ALU.mult).then_inc(sem("decayed"), 1)
            for i in range(2):
                pool.wait_ge(sem("outer_added"), 8 * (i + 1))
                pool.dma_start(outs["gdn_s"][0, 4 * i:4 * i + 4].rearrange("b h d e -> d (b h) e"),
                               ring[:, state_slot[i], :].rearrange("p (a e) -> p a e", e=HD)).then_inc(sem("states_out"), 16)
        out_sems.update(states_out=32)

        def leave(eng, left):
            eng.drain()
            eng.sem_inc(sem(left), 1)
            eng.wait_ge(sem("phase_open"), 1)
            eng.drain()

        def pool_clear(pool):
            pool.wait_ge(sem("delta_mixed"), 1)
            for left in ("act_left", "pe_left", "dve_left", "sp_left"):
                pool.wait_ge(sem(left), 1)
            for name in CLEARED:
                pool.sem_clear(sem(name))
            pool.sem_inc(sem("phase_open"), 1)


        kvr = work[:, 0:3072].rearrange("p (t c d) -> p t c d", t=NT, d=HD)
        kvs = v3(work, 3072, 12, HD)[0:NB]
        dead = [B_GQ * TC]

        def old(n):
            r = pT[:, dead[0]:dead[0] + n]
            dead[0] += n
            assert dead[0] <= NBLK * TC
            return r

        w2b, hpart, hidp, ckTp, cvp, cmpk = old(256), old(256), old(32), old(16), old(256), old(1024)
        cvp3 = cvp.rearrange("p (h d) -> p h d", h=KVH)[0:NCP]
        score = [work[:, 4608 + 520 * i:5128 + 520 * i] for i in range(2)]
        PT = [v3(work, 5648 + 640 * i, 5, P) for i in range(2)]
        stat = [[cols(f"{n}{i}", 3) for i in range(2)] for n in ("top", "total")]
        dist3, cdist3, cseen3 = v3(dist, 0, NT, T), v3(cdist, 0, NT, NCP), v3(cseen, 0, NT, NCP)
        G_W1 = G_NEXT + 2
        N_ATT = NT * HEADS
        slope = [2.0 ** -(h + 1) for h in range(HEADS)]

        def full_at(eng, G):
            eng.wait_ge(full[G % RING], full_base[G % RING] + 16 * (G // RING + 1))

        def pool_att_consts(pool):
            c = sem("att_consts")
            for t in range(NT):
                step(pool, c, pool.iota(dist3[:, t, :], [[-1, T]], base=t * P, channel_multiplier=1, allow_small_or_imprecise_dtypes=True))
                step(pool, c, pool.affine_select(out=dist3[:, t, :], in_=dist3[:, t, :], compare_op=ALU.is_ge, fill=FAR, base=t * P,
                                                 pattern=[[-1, T]], channel_multiplier=1))
                step(pool, c, pool.iota(cdist3[:, t, :], [[-CMP, NCP]], base=t * P - (CMP - 1), channel_multiplier=1,
                                        allow_small_or_imprecise_dtypes=True))
                step(pool, c, pool.affine_select(out=cseen3[:, t, :], in_=ones[:, 0:NCP], compare_op=ALU.is_ge, fill=0.0,
                                                 base=t * P - (CMP - 1), pattern=[[-CMP, NCP]], channel_multiplier=1))
                step(pool, c, pool.affine_select(out=cdist3[:, t, :], in_=cdist3[:, t, :], compare_op=ALU.is_ge, fill=FAR,
                                                 base=t * P - (CMP - 1), pattern=[[-CMP, NCP]], channel_multiplier=1))

        def pool_att(pool):
            for b in range(NB):
                pool.dma_start(outs["win_s"][0, b, 0:WIN - 1].rearrange("(a w) s h d -> a (w s h d)", a=7),
                               io["state_win_kv"][0, b, 1:WIN].rearrange("(a w) s h d -> a (w s h d)", a=7)).then_inc(sem("win_copied"), 16)
            pool.wait_ge(sem("delta_mixed"), 1)
            step(pool, sem("hpart_clear"), pool.memset(hpart, 0.0))
            pool.wait_ge(sem("kv_rows"), 9)
            for i, name in enumerate(("cmp", "sel", "win")):
                pool.dma_start(outs[name + "_p"][0, 0].rearrange("(t p) s h d -> p t (s h d)", p=P),
                               kvr.rearrange("p t c d -> p t (c d)")[:, :, 512 * i:512 * i + 512]).then_inc(sem("kv_out"), 16)
                to = outs[name + "_s"][0, :, 0] if i < 2 else outs["win_s"][0, :, WIN - 1]
                pool.dma_start(to.rearrange("b s h d -> b (s h d)"), kvs.rearrange("p c d -> p (c d)")[:, 512 * i:512 * i + 512]).then_inc(sem("kv_out"), 16)
        out_sems.update(win_copied=16 * NB, kv_out=96)

        def sp_w1(sp):
            for s in range(2):
                sp.wait_ge(sem("proj_sum"), 8 + 52)
                sp.dma_start(ring[:, (G_W1 + s) % RING, :].rearrange("p (l e) -> p l e", e=HD),
                             io["cmp_w1"][0, s].rearrange("l d e -> d l e")).then_inc(full[(G_W1 + s) % RING], 16)

        def sp_w2(sp):
            sp.wait_ge(sem("delta_mixed"), 1)
            sp.dma_start(w2b.rearrange("p (s d) -> p s d", s=2), io["cmp_w2"][0].rearrange("s e d -> e s d")).then_inc(sem("w2b_in"), 16)

        def pe_kv(pe):
            pe.wait_ge(sem("delta_mixed"), 1)
            n = 0
            for t in range(3):
                rows = P if t < 2 else NB
                for i in range(3):
                    if n >= 4:
                        pe.wait_ge(sem("kv_rows"), n - 3)
                    for c in range(4):
                        mm = pe.transpose(bank(n % 4)[0:rows, c * P:(c + 1) * P], pT3[:, 8 + 4 * i + c, t * P:t * P + rows], ident[:])
                    mm.then_inc(sem("kv_T"), 1)
                    n += 1
            pe.wait_ge(sem("cmpk_ready"), 2)
            for s in range(2):
                full_at(pe, G_W1 + s)
                for l4 in range(CMP // 4):
                    for g in range(4):
                        l = 4 * l4 + g
                        mm = pe.matmul(bank(4)[32 * g:32 * g + 16, s * P:(s + 1) * P], cmpk[:, (s * CMP + l) * 16:(s * CMP + l + 1) * 16],
                                       ring[:, (G_W1 + s) % RING, l * HD:(l + 1) * HD], start=l4 == 0, stop=l4 == CMP // 4 - 1)
            mm.then_inc(sem("hpart_sum"), 1)
            pe.wait_ge(sem("hpart_moved"), 1)
            for s in range(2):
                mm = pe.matmul(bank(5)[:, s * 96:(s + 1) * 96], hpart[:, s * P:(s + 1) * P], fold, start=True, stop=True)
            mm.then_inc(sem("hidp_sum"), 1)
            pe.wait_ge(sem("hidp_ready"), 2)
            pe.wait_ge(sem("w2b_in"), 16)
            pe.matmul(bank(6)[:, 0:16], w2b[:, 0:HD], hidp[:, 0:16], start=True, stop=True)
            for h in range(KVH):
                mm = pe.matmul(bank(6)[0:NCP, 128 + h * HD:256 + h * HD], hidp[:, 16 + h * NCP:16 + (h + 1) * NCP], w2b[:, HD:2 * HD],
                               start=True, stop=True)
            mm.then_inc(sem("cmpp_sum"), 1)
            pe.wait_ge(sem("cmpp_moved"), 2)
            pe.wait_ge(sem("q_scaled_att"), 1)

            def scores(i):
                t, h = divmod(i, HEADS)
                kh, nk = h // 4, P * (t + 1)
                q = pT3[:, h, col(t)]
                if i >= 2:
                    pe.wait_ge(sem("score_read"), i - 1)
                pe.matmul(bank(i % 2)[:, 0:nk], q, pT3[:, B_SK + kh, 0:nk], start=True, stop=True)
                pe.matmul(bank(i % 2)[:, nk:2 * nk], q, pT3[:, B_WK + kh, 0:nk], start=True, stop=True)
                pe.matmul(bank(2 + i % 2)[:, 0:NCP], q, ckTp[:, kh * NCP:(kh + 1) * NCP], start=True, stop=True).then_inc(sem("score_mm"), 1)

            scores(0)
            for i in range(N_ATT):
                t, h = divmod(i, HEADS)
                kh, nk = h // 4, P * (t + 1)
                if i + 1 < N_ATT:
                    scores(i + 1)
                s = score[i % 2]
                pe.wait_ge(sem("p_ready"), i + 1)
                if i >= 1:
                    pe.wait_ge(sem("pt_moved"), i)
                for k in range(2 * (t + 1)):
                    pe.transpose(bank(4 + i % 2)[:, k * P:(k + 1) * P], s[:, k * P:(k + 1) * P], ident[:])
                pe.transpose(bank(6)[0:NCP, 0:P], s[:, 512:520], ident[:]).then_inc(sem("pt_T"), 1)
                pe.wait_ge(sem("pt_moved"), i + 1)
                if i >= 1:
                    pe.wait_ge(sem("o_moved"), i)
                for k in range(2 * (t + 1)):
                    br, kt = divmod(k, t + 1)
                    pe.matmul(bank(7)[:, 0:P], kvr[:, kt, (6 if br == 0 else 10) + kh, :], PT[i % 2][:, k, :], start=k == 0, stop=False)
                pe.matmul(bank(7)[:, 0:P], cvp3[:, kh, :], PT[i % 2][0:NCP, 4, :], start=False, stop=True).then_inc(sem("o_mm_att"), 1)

        def act_kv(act):
            act.wait_ge(sem("delta_mixed"), 1)
            act.wait_ge(sem("states_done"), 1)
            n = 0
            for t in range(3):
                rows = P if t < 2 else NB
                for i in range(3):
                    act.wait_ge(sem("kv_T"), n + 1)
                    dst = kvr[:, t, 4 * i:4 * i + 4, :] if t < 2 else kvs[:, 4 * i:4 * i + 4, :]
                    act.activation(dst, v3(bank(n % 4), 0, 4, P)[0:rows], ACT.Copy).then_inc(sem("kv_rows"), 1)
                    n += 1
            act.wait_ge(sem("hidp_sum"), 1)
            for s in range(2):
                act.activation(hidp[:, 16 * s:16 * s + 16], bank(5)[:, 96 * s:96 * s + 16], ACT.Gelu_apprx_tanh,
                               bias=hid_bias[:, s:s + 1]).then_inc(sem("hidp_ready"), 1)
            act.wait_ge(sem("cmpp_sum"), 1)
            act.activation(ckTp, bank(6)[:, 0:16], ACT.Copy).then_inc(sem("cmpp_moved"), 1)
            act.activation(cvp[0:NCP, :], bank(6)[0:NCP, 128:384], ACT.Copy).then_inc(sem("cmpp_moved"), 1)

            def exps(i):
                t = i // HEADS
                nk = P * (t + 1)
                top, total = stat[0][i % 2], stat[1][i % 2]
                act.wait_ge(sem("top_ready"), i + 1)
                for br, sl in ((1, slice(0, nk)), (2, slice(nk, 2 * nk)), (0, slice(512, 520))):
                    act.activation(score[i % 2][:, sl], score[i % 2][:, sl], ACT.Exp, bias=top[:, br:br + 1],
                                   accum_out=total[:, br:br + 1]).then_inc(sem("exp_done"), 1)

            exps(0)
            for i in range(N_ATT):
                if i + 1 < N_ATT:
                    exps(i + 1)
                t = i // HEADS
                act.wait_ge(sem("pt_T"), i + 1)
                if i >= 2:
                    act.wait_ge(sem("o_mm_att"), i - 1)
                act.activation(PT[i % 2][:, 0:2 * (t + 1), :], v3(bank(4 + i % 2), 0, 2 * (t + 1), P), ACT.Copy).then_inc(sem("pt_part"), 1)
                act.activation(PT[i % 2][0:NCP, 4, :], bank(6)[0:NCP, 0:P], ACT.Copy).then_inc(sem("pt_moved"), 1)

        def dve_kv(dve):
            c = sem("att_steps")
            dve.wait_ge(sem("delta_mixed"), 1)
            for s in range(2):
                dve.tensor_copy(v4(cmpk, s * 512, CMP, KVH, NCP), pT3[:, 8 + 2 * s:10 + 2 * s, 0:T].rearrange("p h (n l) -> p l h n", l=CMP)
                                ).then_inc(sem("cmpk_ready"), 1)
            dve.wait_ge(sem("att_consts"), 10)
            dve.tensor_scalar(pT3[:, 0:8, :], pT3[:, 0:8, :], SCALE, None, ALU.mult).then_inc(sem("q_scaled_att"), 1)
            dve.wait_ge(sem("hpart_sum"), 1)
            dve.wait_ge(sem("hpart_clear"), 1)
            for g in range(4):
                mv = dve.tensor_copy(hpart[32 * g:32 * g + 16, :], bank(4)[32 * g:32 * g + 16, 0:256])
            mv.then_inc(sem("hpart_moved"), 1)

            def tops(i):
                t, h = divmod(i, HEADS)
                nk = P * (t + 1)
                s, top = score[i % 2], stat[0][i % 2]
                dve.wait_ge(sem("score_mm"), i + 1)
                if i >= 2:
                    dve.wait_ge(sem("pt_T"), i - 1)
                two = s[:, 0:2 * nk].rearrange("p (a k) -> p a k", a=2)
                step(dve, c, dve.scalar_tensor_tensor(two, B1(dist3[:, t, 0:nk], 2), -slope[h],
                                                      bank(i % 2)[:, 0:2 * nk].rearrange("p (a k) -> p a k", a=2), ALU.mult, ALU.add))
                step(dve, sem("score_read"), dve.scalar_tensor_tensor(s[:, 512:520], cdist3[:, t, :], -slope[h], bank(2 + i % 2)[:, 0:NCP],
                                                                      ALU.mult, ALU.add))
                dve.tensor_reduce(top[:, 1:3], two, AX, ALU.max)
                step(dve, c, dve.tensor_reduce(top[:, 0:1], s[:, 512:520], AX, ALU.max))
                step(dve, sem("top_ready"), dve.tensor_scalar(top, top, -1.0, None, ALU.mult))

            tops(0)
            for i in range(N_ATT):
                t, h = divmod(i, HEADS)
                nk = P * (t + 1)
                if i + 1 < N_ATT:
                    tops(i + 1)
                s, total = score[i % 2], stat[1][i % 2]
                dve.wait_ge(sem("exp_done"), 3 * (i + 1))
                step(dve, c, dve.reciprocal(total, total))
                step(dve, c, dve.tensor_tensor(total, total, gates[:, t * 24 + 3 * h:t * 24 + 3 * h + 3], ALU.mult))
                two = s[:, 0:2 * nk].rearrange("p (a k) -> p a k", a=2)
                dve.tensor_tensor(two, two, B2(total[:, 1:3], nk), ALU.mult)
                dve.scalar_tensor_tensor(s[:, 512:520], s[:, 512:520], total[:, 0:1], cseen3[:, t, :], ALU.mult, ALU.mult).then_inc(sem("p_ready"), 1)
                dve.wait_ge(sem("o_mm_att"), i + 1)
                dve.tensor_copy(mix3[:, h, col(t)], bank(7)[:, 0:P]).then_inc(sem("o_moved"), 1)

        def sp_states_stored(sp):
            sp.wait_ge(sem("states_out"), 32)
            sp.sem_inc(sem("states_done"), 1)

        ssel, swin, scmp = work[0:ROWS, 0:PAST + 1], work[0:ROWS, 2112:2112 + WIN + 1], work[0:ROWS, 2628:2692]
        gsel, gselT, sel_b = work[0:ROWS, 2692:2708], work[0:16, 2708:2772], work[0:NB, 2772:2836]
        sel_bh = [work[0:NB, 2836:2900], work[0:NB, 2900:2964]]
        headmask, gatesel = work[0:ROWS, 2964:2972], work[0:ROWS, 2972:2996]
        KT = v3(work, 4608, 4, 512)
        PTc = work[0:NC, 6656:6720]
        ndiag = [work[0:ROWS, 6720:6784], work[0:ROWS, 6784:6848]]
        vnew = [work[0:ROWS, 6848:6976], work[0:ROWS, 6976:7104]]
        dead[0] -= 1024
        qpad, sdist, wdist, endist = old(PAIRS * 68), old(PAST)[0:ROWS], old(WIN)[0:ROWS], old(NC)[0:ROWS]
        PTs, PTw = old(PAGES * 96), old(4 * 96)
        PTs3, PTw3 = PTs.rearrange("p (k c) -> p k c", c=96), PTw.rearrange("p (k c) -> p k c", c=96)
        tri = old(NSEL * NSEL)[0:PAIRS].rearrange("p (a b) -> p a b", b=NSEL)
        beats = PTs[0:PAIRS, 0:NSEL * NSEL].rearrange("p (a b) -> p a b", b=NSEL)
        unfold = [old(96), old(96)]
        pvs = [old(256), old(256)]
        pvw = work[:, 4608:4608 + NB * 256]
        nslope, sgate = cols("nslope", 1)[0:ROWS], cols("sgate", 3)[0:ROWS]
        stop_, stotal = cols("stop", 3)[0:ROWS], cols("stotal", 3)[0:ROWS]
        s33, rank1, rank2 = (cols(n, NSEL)[0:PAIRS] for n in ("s33", "rank1", "rank2"))
        sbias = cols("sbias", NSEL)[0:ROWS]
        G_ATT = G_NEXT + 4
        N_ITEMS, selected = 20, lambda m: 2 <= m < 10 or m >= 12
        item_full, at_ = [], [full_base[j] + 16 * len(range(j, G_ATT, RING)) for j in range(RING)]
        for m in range(N_ITEMS):
            at_[(G_ATT + m) % RING] += 16 * PAGES if selected(m) else 16
            item_full.append(at_[(G_ATT + m) % RING])
        G_OUT = G_ATT + N_ITEMS
        full_base2 = [at_[j] - 16 * len(range(j, G_OUT, RING)) for j in range(RING)]

        def sp_samp(sp):
            win = io["state_win_kv"][0].rearrange("b (t p) s h d -> p (b t) s (h d)", p=P)
            for m in range(N_ITEMS):
                j = (G_ATT + m) % RING
                if m in (2, 3):
                    sp.wait_ge(sem("hpart_sum"), 1)
                elif m >= 4:
                    sp.wait_ge(sem("item_used"), m - 3)
                kv = 0 if m < 10 else 1
                if selected(m):
                    b = m - (2 if m < 10 else 12)
                    for pp in range(PAGES):
                        page = sp.value_load(pagesb[0:1, b * PAGES + pp:b * PAGES + pp + 1], min_val=0, max_val=NPHYS - 1)
                        sp.dma_start(ring[:, j, pp * 256:(pp + 1) * 256],
                                     io["cache_sel_kv"][0, bass.ds(page, 1), :, kv].rearrange("a t h d -> (a t) (h d)")).then_inc(full[j], 16)
                else:
                    i = m % 2
                    sp.dma_start(ring[:, j, :].rearrange("p (a c) -> p a c", c=256), win[:, 16 * i:16 * i + 16, kv]).then_inc(full[j], 16)

        def pool_samp(pool):
            c = sem("samp_consts")
            pool.wait_ge(sem("hpart_sum"), 1)
            step(pool, c, pool.memset(qpad, 0.0))
            step(pool, c, pool.memset(tri, 1.0))
            step(pool, c, pool.affine_select(out=tri, in_=tri, compare_op=ALU.is_gt, fill=0.0, base=0,
                                             pattern=[[1, NSEL], [-1, NSEL]], channel_multiplier=0))
            step(pool, c, pool.iota(sdist, [[-1, PAST]], base=PAST, channel_multiplier=0, allow_small_or_imprecise_dtypes=True))
            step(pool, c, pool.iota(wdist, [[-1, WIN]], base=WIN, channel_multiplier=0, allow_small_or_imprecise_dtypes=True))
            step(pool, c, pool.memset(wdist[:, 0:1], FAR))
            step(pool, c, pool.iota(endist, [[-CMP, NC]], base=PAST - (CMP - 1), channel_multiplier=0, allow_small_or_imprecise_dtypes=True))
            step(pool, c, pool.iota(nslope.bitcast(I32), [[0, 1]], base=0, channel_multiplier=1))
            step(pool, c, pool.memset(PTw, 0.0))
            step(pool, c, pool.memset(unfold[0], 0.0))
            step(pool, c, pool.memset(unfold[1], 0.0))
            pool.wait_ge(sem("o_mm_att"), N_ATT)
            pool.wait_ge(sem("kv_out"), 96)
            step(pool, c, pool.memset(sel_bh[0], 0.0))
            step(pool, c, pool.memset(sel_bh[1], 0.0))
            pool.wait_ge(sem("ranked"), 1)
            pool.memset(PTs, 0.0).then_inc(sem("pts_clear"), 1)

        def dve_samp(dve):
            c = sem("samp_steps")
            dve.wait_ge(sem("samp_consts"), 8)
            x = nslope.bitcast(I32)
            step(dve, c, dve.tensor_scalar(x, x, 7, None, ALU.bitwise_and))
            step(dve, c, dve.tensor_scalar(x, x, -1, 126, ALU.mult, ALU.add))
            step(dve, c, dve.tensor_scalar(x, x, 23, None, ALU.logical_shift_left))
            step(dve, c, dve.tensor_scalar(nslope, nslope, -1.0, None, ALU.mult))
            dve.wait_ge(sem("samp_consts"), 13)
            dve.wait_ge(sem("o_mm_att"), N_ATT)
            dve.wait_ge(sem("kv_out"), 96)
            i64 = ident[0:ROWS, 0:ROWS]
            step(dve, c, dve.tensor_reduce(headmask, i64.rearrange("p (b c) -> p c b", b=NB), AX, ALU.add))
            step(dve, c, dve.tensor_reduce(gsel, i64.rearrange("p (q g) -> p q g", g=4), AX, ALU.add))
            step(dve, c, dve.tensor_copy(gselT.rearrange("p (q g) -> p q g", g=4), B2(ident[0:16, 0:16], 4)))
            step(dve, c, dve.tensor_copy(sel_b.rearrange("p (b c) -> p b c", b=NB), B2(ident[0:NB, 0:NB], 8)))
            for h in range(KVH):
                step(dve, c, dve.tensor_copy(sel_bh[h].rearrange("p (b c) -> p b c", b=NB)[:, :, 4 * h:4 * h + 4], B2(ident[0:NB, 0:NB], 4)))
                for g in range(4):
                    step(dve, c, dve.tensor_copy(unfold[h][32 * g:32 * g + 8, 4 * h:4 * h + 4],
                                                 ident[32 * g:32 * g + 8, 32 * g + 4 * h:32 * g + 4 * h + 4]))
            dve.tensor_copy(qpad.rearrange("p (a k c) -> p a k c", k=KVH, c=68)[:, :, :, 0:4],
                            pT3[:, 0:8, T:TC].rearrange("p (k g) b -> p b k g", k=KVH)).then_inc(sem("samp_ready"), 1)
            dve.wait_ge(sem("scmp_mm"), 1)
            step(dve, c, dve.tensor_tensor(gatesel.rearrange("p (r h) -> p r h", r=3), bank(7)[0:ROWS, 0:24].rearrange("p (h r) -> p r h", r=3),
                                           B1(headmask, 3), ALU.mult))
            step(dve, c, dve.tensor_reduce(sgate, gatesel.rearrange("p (r h) -> p r h", r=3), AX, ALU.add))
            step(dve, c, dve.scalar_tensor_tensor(scmp, endist, nslope, bank(7)[0:ROWS, 64:128], ALU.mult, ALU.add))
            step(dve, c, dve.tensor_reduce(stop_[:, 0:1], scmp, AX, ALU.max))
            dve.tensor_scalar(stop_[:, 0:1], stop_[:, 0:1], -1.0, None, ALU.mult).then_inc(sem("samp_top"), 1)
            dve.wait_ge(sem("samp_exp"), 1)
            step(dve, c, dve.reciprocal(stotal[:, 0:1], stotal[:, 0:1]))
            dve.tensor_scalar(scmp, scmp, stotal[:, 0:1], None, ALU.mult).then_inc(sem("pc_ready"), 1)

            def moves(lo, hi):
                for n in range(lo, hi, 2):
                    dve.wait_ge(sem("kt_T"), n + 1)
                    if n >= 4:
                        dve.wait_ge(sem("kt_used"), n - 3)
                    dve.tensor_copy(KT[:, n % 4, :], bank(5)).then_inc(sem("kt_even"), 1)

            moves(0, 32)
            dve.wait_ge(sem("imp_mm"), 1)
            step(dve, c, dve.tensor_reduce(s33[:, 0:NC // 2], bank(7)[0:PAIRS, 128:192].rearrange("p (a b) -> p a b", b=2), AX, ALU.add))
            step(dve, c, dve.memset(s33[:, 0:1], FORCE))
            step(dve, c, dve.memset(s33[:, NSEL - 2:NSEL], FORCE))
            step(dve, c, dve.tensor_tensor(beats, B1(s33, NSEL), B2(s33, NSEL), ALU.is_gt))
            step(dve, c, dve.tensor_reduce(rank1, beats, AX, ALU.add))
            step(dve, c, dve.tensor_tensor(beats, B1(s33, NSEL), B2(s33, NSEL), ALU.is_equal))
            step(dve, c, dve.tensor_tensor(beats, beats, tri, ALU.mult))
            step(dve, c, dve.tensor_reduce(rank2, beats, AX, ALU.add))
            step(dve, c, dve.tensor_tensor(rank1, rank1, rank2, ALU.add))
            step(dve, sem("ranked"), dve.tensor_scalar(rank1, rank1, float(TOPN), None, ALU.is_lt))
            moves(32, 80)
            dve.wait_ge(sem("picked_mm"), 1)
            step(dve, c, dve.tensor_scalar(sbias, bank(7)[0:ROWS, 192:192 + NSEL], 1.0, BIG, ALU.subtract, ALU.mult))
            step(dve, c, dve.tensor_scalar(swin[:, WIN:], bank(7)[0:ROWS, 257:258], 1.0, None, ALU.mult))
            step(dve, c, dve.tensor_tensor(ssel[:, PAST:], bank(7)[0:ROWS, 256:257], sbias[:, NSEL - 1:], ALU.add))
            step(dve, c, dve.scalar_tensor_tensor(swin[:, 0:WIN], wdist, nslope, bank(4)[0:ROWS, :], ALU.mult, ALU.add))
            step(dve, c, dve.tensor_reduce(stop_[:, 2:3], swin, AX, ALU.max))
            step(dve, c, dve.scalar_tensor_tensor(ssel[:, 0:PAST].rearrange("p (a b) -> p a b", b=512), sdist.rearrange("p (a b) -> p a b", b=512),
                                                  nslope, ps[0:ROWS, 0:4, :], ALU.mult, ALU.add))
            blocks = ssel[:, 0:PAST].rearrange("p (a b) -> p a b", b=SEL)
            step(dve, c, dve.tensor_tensor(blocks, blocks, B2(sbias[:, 0:NSEL - 1], SEL), ALU.add))
            step(dve, c, dve.tensor_reduce(stop_[:, 1:2], ssel, AX, ALU.max))
            dve.tensor_scalar(stop_[:, 1:3], stop_[:, 1:3], -1.0, None, ALU.mult).then_inc(sem("samp_top"), 1)
            step(dve, c, dve.tensor_scalar(scmp, scmp, sgate[:, 0:1], None, ALU.mult))
            dve.wait_ge(sem("samp_exp"), 3)
            step(dve, c, dve.reciprocal(stotal[:, 1:3], stotal[:, 1:3]))
            step(dve, c, dve.tensor_tensor(stotal[:, 1:3], stotal[:, 1:3], sgate[:, 1:3], ALU.mult))
            step(dve, c, dve.tensor_scalar(swin, swin, stotal[:, 2:3], None, ALU.mult))
            step(dve, c, dve.tensor_scalar(ssel, ssel, stotal[:, 1:2], None, ALU.mult))
            step(dve, c, dve.tensor_scalar(ndiag[0], i64, ssel[:, PAST:], None, ALU.mult))
            dve.tensor_scalar(ndiag[1], i64, swin[:, WIN:], None, ALU.mult).then_inc(sem("samp_p"), 1)
            dve.wait_ge(sem("samp_pT"), 1)
            dve.wait_ge(sem("pts_clear"), 1)
            dve.tensor_copy(PTs3[:, 0:8, 0:ROWS], v3(bank(5), 0, 8, ROWS)).then_inc(sem("samp_pt_dve"), 1)
            dve.wait_ge(sem("samp_folded"), 1)
            o8 = mix3[:, 0:8, T:TC]
            fold_v = lambda i: v3(bank(2 + i), 0, 4, 96)[:, :, 0:8].rearrange("p b h -> p h b")
            rows_v = lambda i: bank(i)[:, 0:ROWS].rearrange("p (b h) -> p h b", h=HEADS)
            for i in range(2):
                step(dve, c, dve.tensor_copy(o8[:, :, 4 * i:4 * i + 4], fold_v(i)))
            step(dve, c, dve.tensor_tensor(o8, o8, rows_v(6), ALU.add))
            dve.tensor_tensor(o8, o8, rows_v(4), ALU.add).then_inc(sem("samp_mixed"), 1)

        def act_samp(act):
            act.wait_ge(sem("samp_top"), 1)
            act.activation(scmp, scmp, ACT.Exp, bias=stop_[:, 0:1], accum_out=stotal[:, 0:1]).then_inc(sem("samp_exp"), 1)
            for n in range(1, 80, 2):
                act.wait_ge(sem("kt_T"), n + 1)
                if n >= 4:
                    act.wait_ge(sem("kt_used"), n - 3)
                act.activation(KT[:, n % 4, :], bank(6), ACT.Copy).then_inc(sem("kt_odd"), 1)
            act.wait_ge(sem("samp_top"), 2)
            act.activation(swin, swin, ACT.Exp, bias=stop_[:, 2:3], accum_out=stotal[:, 2:3]).then_inc(sem("samp_exp"), 1)
            act.activation(ssel, ssel, ACT.Exp, bias=stop_[:, 1:2], accum_out=stotal[:, 1:2]).then_inc(sem("samp_exp"), 1)
            act.wait_ge(sem("samp_pT"), 2)
            act.wait_ge(sem("pts_clear"), 1)
            act.activation(PTs3[:, 8:16, 0:ROWS], v3(bank(6), 0, 8, ROWS), ACT.Copy).then_inc(sem("samp_pt_act"), 1)
            act.activation(PTw3[:, :, 0:ROWS], v3(bank(7), 0, 4, ROWS), ACT.Copy).then_inc(sem("samp_pt_act"), 1)
            act.activation(PTc, bank(7)[0:NC, 256:320], ACT.Copy).then_inc(sem("samp_pt_act"), 1)
            act.wait_ge(sem("vnew_mm"), 1)
            for i in range(2):
                act.activation(vnew[i], bank(7)[0:ROWS, 128 * i:128 * i + 128], ACT.Copy).then_inc(sem("vnew_moved"), 1)
            for n in range(2 * NB):
                act.wait_ge(sem("pv_mm"), n + 1)
                if n >= NB + 2:
                    act.wait_ge(sem("pv_used"), n - NB - 1)
                act.activation(pvw[:, 256 * n:256 * n + 256] if n < NB else pvs[n % 2], bank(n % 2)[:, 0:256], ACT.Copy).then_inc(sem("pv_moved"), 1)

        def pe_samp(pe):
            pair_q = lambda p: qpad[:, 64 * p:64 * p + 64]
            bh_of = lambda p: divmod(p, KVH)
            pe.wait_ge(sem("samp_ready"), 1)
            pe.wait_ge(sem("o_moved"), N_ATT)
            pe.matmul(bank(7)[0:ROWS, 0:24], sel_b, gates[0:NB, 48:72], start=True, stop=True)
            for p in range(PAIRS):
                mm = pe.matmul(bank(7)[0:ROWS, 64:128], pair_q(p), ckT[:, NC * p:NC * (p + 1)], start=p == 0, stop=p == PAIRS - 1)
            for i, blk in enumerate((B_SK, B_WK)):
                for p in range(PAIRS):
                    b, h = bh_of(p)
                    mm = pe.matmul(bank(7)[0:ROWS, 256 + i:257 + i], pair_q(p), pT3[:, blk + h, T + b:T + b + 1], start=p == 0, stop=p == PAIRS - 1)
            mm.then_inc(sem("scmp_mm"), 1)

            def where(n):
                if n < 16:
                    b, h = bh_of(n)
                    return b // 4, lambda k: ((b % 4) * 4 + k) * 256 + h * P, n, 4
                p, q = divmod(n - 16, 4)
                b, h = bh_of(p)
                return 2 + b, lambda k: (4 * q + k) * 256 + h * P, p, q

            def turn(n):
                m, col_, p, bk = where(n)
                pe.wait_ge(full[(G_ATT + m) % RING], item_full[m])
                if n >= 2:
                    pe.wait_ge(sem("kt_odd" if n % 2 else "kt_even"), n // 2)
                for k in range(4):
                    mm = pe.transpose(bank(5 + n % 2)[:, k * P:(k + 1) * P], ring[:, (G_ATT + m) % RING, col_(k):col_(k) + P], ident[:])
                mm.then_inc(sem("kt_T"), 1)
                if n + 1 == 80 or where(n + 1)[0] != m:
                    pe.wait_ge(sem("kt_T"), n + 1)
                    pe.sem_inc(sem("item_used"), 1)

            turn(0)
            for n in range(80):
                if n + 1 < 80:
                    turn(n + 1)
                if n == 20:
                    pe.wait_ge(sem("pc_ready"), 1)
                    pe.matmul(bank(7)[0:PAIRS, 128:192], gsel, scmp, start=True, stop=True).then_inc(sem("imp_mm"), 1)
                m, col_, p, bk = where(n)
                pe.wait_ge(sem("kt_odd" if n % 2 else "kt_even"), n // 2 + 1)
                pe.matmul(bank(bk)[0:ROWS, :], pair_q(p), KT[:, n % 4, :], start=p == 0, stop=p == PAIRS - 1).then_inc(sem("kt_used"), 1)
            pe.wait_ge(sem("ranked"), 1)
            pe.matmul(bank(7)[0:ROWS, 192:192 + NSEL], gselT, rank1, start=True, stop=True).then_inc(sem("picked_mm"), 1)
            pe.wait_ge(sem("samp_p"), 1)
            i64 = ident[0:ROWS, 0:ROWS]
            for k in range(PAGES):
                mm = pe.transpose(bank(5 + k // 8)[:, (k % 8) * ROWS:(k % 8 + 1) * ROWS], ssel[:, k * P:(k + 1) * P], i64)
                if k == 7:
                    mm.then_inc(sem("samp_pT"), 1)
            for k in range(4):
                pe.transpose(bank(7)[:, k * ROWS:(k + 1) * ROWS], swin[:, k * P:(k + 1) * P], i64)
            pe.transpose(bank(7)[0:NC, 256:320], scmp, i64).then_inc(sem("samp_pT"), 1)
            pe.wait_ge(sem("samp_pt_act"), 3)
            pe.wait_ge(sem("samp_pt_dve"), 1)
            for i, first in enumerate((6, 10)):
                for h in range(KVH):
                    mm = pe.matmul(bank(7)[0:ROWS, 128 * i:128 * i + 128], sel_bh[h], kvs[:, first + h, :], start=h == 0, stop=h == 1)
            mm.then_inc(sem("vnew_mm"), 1)
            for p in range(PAIRS):
                pe.matmul(bank(4)[:, 4 * p:4 * p + 4], cvR[:, P * p:P * (p + 1)], PTc[:, 4 * p:4 * p + 4], start=True, stop=True)
            pe.wait_ge(sem("vnew_moved"), 2)
            for i in range(2):
                pe.matmul(bank(6)[:, 0:ROWS], vnew[i], ndiag[i], start=i == 0, stop=i == 1)

            def values(n):
                b, sel_ = n % NB, n >= NB
                m = 12 + b if sel_ else 10 + b // 4
                pe.wait_ge(full[(G_ATT + m) % RING], item_full[m])
                if n >= 2:
                    pe.wait_ge(sem("pv_moved"), n - 1)
                weights, first, count = (PTs3, 0, PAGES) if sel_ else (PTw3, (b % 4) * 4, 4)
                for k in range(count):
                    g = k % 4
                    mm = pe.matmul(bank(n % 2)[32 * g:32 * g + 32, 0:256], weights[:, k, 8 * b:8 * b + 32],
                                   ring[:, (G_ATT + m) % RING, (first + k) * 256:(first + k + 1) * 256], start=k < 4, stop=k >= count - 4)
                mm.then_inc(sem("pv_mm"), 1)
                if sel_ or b % 4 == 3:
                    pe.wait_ge(sem("pv_mm"), n + 1)
                    pe.sem_inc(sem("item_used"), 1)

            def folds(b):
                pe.wait_ge(sem("pv_moved"), NB + b + 1)
                out = bank(2 + b // 4)[:, (b % 4) * 96:(b % 4 + 1) * 96]
                srcs = [(pvw[:, 256 * b + P * h:256 * b + P * (h + 1)], h) for h in range(KVH)]
                srcs += [(pvs[b % 2][:, P * h:P * (h + 1)], h) for h in range(KVH)]
                for i, (s, h) in enumerate(srcs):
                    mm = pe.matmul(out, s, unfold[h], start=i == 0, stop=i == 3)
                mm.then_inc(sem("pv_used"), 1)

            for n in range(2 * NB):
                values(n)
                if n > NB:
                    folds(n - NB - 1)
            folds(NB - 1)
            pe.wait_ge(sem("pv_used"), NB)
            pe.sem_inc(sem("samp_folded"), 1)


        raw3 = v3(pT, 0, KD, TC)

        def sp_out(sp):
            for m in range(4):
                sp.wait_ge(sem("item_used"), N_ITEMS - 3 + m)
                j = (G_OUT + m) % RING
                sp.dma_start(ring[:, j, :].rearrange("p (k n) -> p k n", k=KD), item_src(io["w_out"][0], 256 * m)).then_inc(full[j], 16)
            sp_project(sp, G_OUT + 4, 60, 4, io["w_out"][0], 1024)
            sp_project(sp, G_OUT + 8, 68, 8, io["peer_wq"][0], 0)

        def pe_out(pe):
            pe.wait_ge(sem("samp_mixed"), 1)
            pe_project(pe, G_OUT, 52, 8, mix3, full_base2)
            pe_norm(pe, 2)
            pe_wait_proj_rows(pe, 2)
            pe_project(pe, G_OUT + 8, 68, 8, hT3, full_base2)

        def dve_out(dve):
            c = sem("norm_steps")
            dve_project(dve, 52, 8, pT, 0)
            dve.wait_ge(sem("proj_moved"), 2 + 68)
            for k in range(KD):
                dve.scalar_tensor_tensor(xT3[:, k, 0:T], raw3[:, k, 0:T], mod3[:, M_G1 + k, 0:1], xT3[:, k, 0:T], ALU.mult, ALU.add
                                         ).then_inc(sem("x1_ready"), 1)
            step(dve, c, dve.tensor_tensor(raw3[:, :, T:TC], raw3[:, :, T:TC], mod3[:, M_G1:M_G1 + KD, 1:9], ALU.mult))
            dve.tensor_tensor(xT3[:, :, T:TC], xT3[:, :, T:TC], raw3[:, :, T:TC], ALU.add).then_inc(sem("x1_ready"), 1)
            dve.wait_ge(sem("x1_ready"), KD + 1)
            dve_norm(dve, 2, norm2T, M_SH2, M_SC2)
            dve_project(dve, 68, 8, pT, 0)

        def act_out(act):
            act_norm(act, 2, lambda a: a.wait_ge(sem("x1_ready"), KD + 1))


        qT3 = raw3
        h2r, x1r = v3(pT, KD * TC, NT, D), v3(pT, KD * TC + NT * D, NT, D)
        x1s, h2s = hT[0:NB, 0:D], hT[0:NB, D:2 * D]
        g2s = pT[0:NB, 0:D]
        products = pT[:, D:2 * D]
        g2B, fnB = xT[:, 0:D], xT[:, D:2 * D]
        TAIL = KD * TC + 2 * NT * D
        one_row = pT[0:NB, TAIL:TAIL + NB * P].rearrange("p (b c) -> p b c", c=P)
        unit = v3(pT, TAIL + NB * P, NB, NB)
        wpad = v3(pT, TAIL + NB * P + 64, 2, NB)
        zrow = pT[0:1, TAIL + NB * P + 80:TAIL + NB * P + 80 + P]
        ks3 = v3(work, 0, 2 * HEADS, NKEYS)
        pick = v4(work, 0, HEADS, TOPK, TOPK)
        cand = v4(work, 2048, HEADS, TOPK, TOPK)
        keyrow = v3(work, 2048, 2, P)
        U_ = lambda a, n: work[:, a:a + n]
        keysT, topv, topi, topf = v3(work, 4096, 2, P), v3(work, 4352, 16, TOPK), v3(work, 4608, 16, TOPK), v3(work, 4864, 16, TOPK)
        bestv, bestj, jf, ja, jb = (v3(work, 5120 + 128 * i, HEADS, TOPK) for i in range(5))
        ia, ib = v3(work, 5760, HEADS, TOPK), v3(work, 5888, HEADS, TOPK)
        iota16 = U_(6016, TOPK)
        esum = U_(6032, HEADS)
        eid, egate = U_(6064, NT * SLOTS), U_(6320, NT * SLOTS)
        diag = v3(work, 6576, 4, P)
        idx16, gate16 = v3(work, 7088, 2, TOPK), v3(work, 7120, 2, TOPK)
        dots, gel = cols("dots", 2 * TOPK), cols("gel", 2 * TOPK)
        eid_s, egate_s = cols("eid_s", NB), cols("egate_s", NB)
        eidf_s = work[0:NB, 5504:5632]
        sumsq, yroot = cols("sumsq", 3), cols("yroot", 3)
        U32v = lambda ap: ap.bitcast(U32)
        I32v = lambda ap: ap.bitcast(I32)
        rows_of = (P, P, NB)
        LOWEST = -3e38

        def dve_top(dve, t):
            c = sem("top_steps")
            r = rows_of[t]
            dve.wait_ge(sem("keyscores"), 4 * (t + 1))

            def top16(values, indices, src, last):
                step(dve, c, dve.max(out=values[:, 0:8], in_=src))
                step(dve, c, dve.max_index(out=U32v(indices[:, 0:8]), in_max=values[:, 0:8], in_values=src))
                step(dve, c, dve.match_replace(out=src, in_to_replace=values[:, 0:8], in_values=src, imm_value=LOWEST))
                step(dve, c, dve.max(out=values[:, 8:16], in_=src))
                step(dve, c, dve.max_index(out=U32v(indices[:, 8:16]), in_max=values[:, 8:16], in_values=src))

            for a in range(2 * HEADS):
                top16(topv[0:r, a], topi[0:r, a], ks3[0:r, a], a)
            step(dve, c, dve.tensor_copy(topf[0:r], U32v(topi[0:r])))
            for h in range(HEADS):
                step(dve, c, dve.tensor_tensor(cand[0:r, h], B2(topv[0:r, 2 * h], TOPK), B1(topv[0:r, 2 * h + 1], TOPK), ALU.add))
                top16(bestv[0:r, h], bestj[0:r, h], cand[0:r, h].rearrange("p a b -> p (a b)"), h)
            step(dve, c, dve.tensor_copy(esum[0:r], bestv[0:r, :, 0]))
            dve.tensor_tensor(bestv[0:r], bestv[0:r], B2(esum[0:r], TOPK), ALU.subtract).then_inc(sem("top_diff"), 1)
            ji = I32v(bestj[0:r])
            step(dve, c, dve.tensor_scalar(I32v(jf[0:r]), ji, 4, None, ALU.logical_shift_right))
            step(dve, c, dve.tensor_copy(ja[0:r], I32v(jf[0:r])))
            step(dve, c, dve.tensor_scalar(I32v(jf[0:r]), ji, 15, None, ALU.bitwise_and))
            step(dve, c, dve.tensor_copy(jb[0:r], I32v(jf[0:r])))
            for half, (j_, i_) in enumerate(((ja, ia), (jb, ib))):
                step(dve, c, dve.tensor_tensor(pick[0:r], j_[0:r].unsqueeze(3).to_broadcast([r, HEADS, TOPK, TOPK]),
                                               iota16[0:r].unsqueeze(1).unsqueeze(1).to_broadcast([r, HEADS, TOPK, TOPK]), ALU.is_equal))
                keys_ = topf[0:r].rearrange("p (h a) k -> p h a k", a=2)[:, :, half, :]
                step(dve, c, dve.tensor_tensor(pick[0:r], pick[0:r], keys_.unsqueeze(2).to_broadcast([r, HEADS, TOPK, TOPK]), ALU.mult))
                step(dve, c, dve.tensor_reduce(i_[0:r], pick[0:r], AX, ALU.add))
            if t < NT:
                out_e = I32v(eid[:, t * SLOTS:(t + 1) * SLOTS].rearrange("p (h k) -> p h k", k=TOPK))
                out_g = egate[:, t * SLOTS:(t + 1) * SLOTS].rearrange("p (h k) -> p h k", k=TOPK)
            else:
                out_e = eidf_s.rearrange("p (h k) -> p h k", k=TOPK)
                out_g = bestv[0:r]
            step(dve, c, dve.scalar_tensor_tensor(out_e, ia[0:r], float(NKEYS), ib[0:r], ALU.mult, ALU.add))
            dve.wait_ge(sem("best_exp"), t + 1)
            step(dve, c, dve.tensor_reduce(esum[0:r], bestv[0:r], AX, ALU.add))
            step(dve, c, dve.reciprocal(esum[0:r], esum[0:r]))
            dve.tensor_tensor(out_g, bestv[0:r], B2(esum[0:r], TOPK), ALU.mult).then_inc(sem("experts_ready"), 1)
            dve.wait_ge(sem("experts_ready"), t + 1)

        def act_peer(act):
            act.dma_start(keyrow, io["peer_keys"][0].rearrange("a k d -> k a d")).then_inc(sem("keys_in"), 16)
            act.wait_ge(sem("keys_T"), 1)
            act.activation(keysT, v3(bank(7), 0, 2, P), ACT.Copy).then_inc(sem("keys_ready"), 1)

            def scores(t):
                r = rows_of[t]
                act.wait_ge(sem("keyscore_mm"), t + 1)
                if t:
                    act.wait_ge(sem("experts_ready"), t)
                for q in range(4):
                    act.activation(ks3[0:r, 4 * q:4 * q + 4, :], v3(bank(q), 0, 4, P)[0:r], ACT.Copy).then_inc(sem("keyscores"), 1)

            def exps(t):
                r = rows_of[t]
                act.wait_ge(sem("top_diff"), t + 1)
                act.activation(bestv[0:r], bestv[0:r], ACT.Exp).then_inc(sem("best_exp"), 1)

            scores(0)
            n = 0
            for t in range(NT):
                for q in range(4):
                    act.wait_ge(sem("rows_mm"), n + 1)
                    act.activation(h2r[:, t, 512 * q:512 * q + 512], bank(4 + n % 2), ACT.Copy).then_inc(sem("rows_out"), 1)
                    n += 1
            for q in range(4):
                act.wait_ge(sem("rows_mm"), 12)
                act.activation(h2s[:, 512 * q:512 * q + 512], bank(4 + q)[0:NB, :], ACT.Copy).then_inc(sem("rows_out"), 1)
            n = 12
            for t in range(NT + 1):
                for q in range(4):
                    act.wait_ge(sem("rows_mm"), n + 1)
                    dst = x1r[:, t, 512 * q:512 * q + 512] if t < NT else x1s[:, 512 * q:512 * q + 512]
                    act.activation(dst, bank(4 + n % 2)[0:rows_of[t], :], ACT.Copy).then_inc(sem("rows_out"), 1)
                    n += 1
            for q in range(8):
                for i in range(4):
                    k = 4 * (q % 4) + i
                    if q:
                        act.wait_ge(sem("spread_mm"), q)
                    act.activation(diag[:, i, :], ident[:], ACT.Copy,
                                   scale=mod3[:, M_G2 + k, 0:1] if q < 4 else finalT[:, k:k + 1]).then_inc(sem("spread_diag"), 1)
                act.wait_ge(sem("spread_mm"), q + 1)
                act.activation((g2B if q < 4 else fnB)[:, 512 * (q % 4):512 * (q % 4) + 512], bank(4 + q % 2), ACT.Copy).then_inc(sem("spread"), 1)
            exps(0)
            scores(1)
            exps(1)
            scores(2)
            for q in range(4):
                act.wait_ge(sem("g2_mm"), q + 1)
                act.activation(g2s[:, 512 * q:512 * q + 512], bank(4 + q)[0:NB, :], ACT.Copy).then_inc(sem("g2_rows"), 1)
            exps(2)

        def pe_peer(pe):
            pe.wait_ge(sem("proj_moved"), 2 + 84)
            pe.wait_ge(sem("keys_in"), 16)
            for i in range(2):
                mm = pe.transpose(bank(7)[:, i * P:(i + 1) * P], keyrow[:, i, :], ident[:])
            mm.then_inc(sem("keys_T"), 1)
            pe.wait_ge(sem("keys_ready"), 1)

            def scores(t):
                if t:
                    pe.wait_ge(sem("keyscores"), 4 * t)
                for a in range(2 * HEADS):
                    mm = pe.matmul(bank(a // 4)[0:rows_of[t], (a % 4) * P:(a % 4 + 1) * P], qT3[:, a, t * P:t * P + rows_of[t]],
                                   keysT[:, a % 2, :], start=True, stop=True)
                mm.then_inc(sem("keyscore_mm"), 1)

            def rows(src, t, q, bk):
                for i in range(4):
                    mm = pe.transpose(bank(bk)[0:rows_of[t], i * P:(i + 1) * P], src[:, 4 * q + i, t * P:t * P + rows_of[t]], ident[:])
                mm.then_inc(sem("rows_mm"), 1)

            scores(0)
            n = 0
            for t in range(NT):
                for q in range(4):
                    if n >= 2:
                        pe.wait_ge(sem("rows_out"), n - 1)
                    rows(hT3, t, q, 4 + n % 2)
                    n += 1
            pe.wait_ge(sem("rows_out"), 8)
            for q in range(4):
                rows(hT3, NT, q, 4 + q)
            pe.wait_ge(sem("rows_out"), 12)
            n = 12
            for t in range(NT + 1):
                for q in range(4):
                    if n >= 14:
                        pe.wait_ge(sem("rows_out"), n - 1)
                    rows(xT3, t, q, 4 + n % 2)
                    n += 1
            pe.wait_ge(sem("rows_out"), 24)
            for q in range(8):
                pe.wait_ge(sem("spread_diag"), 4 * q + 4)
                if q >= 2:
                    pe.wait_ge(sem("spread"), q - 1)
                for i in range(4):
                    mm = pe.matmul(bank(4 + q % 2)[:, i * P:(i + 1) * P], ones[:], diag[:, i, :], start=True, stop=True)
                mm.then_inc(sem("spread_mm"), 1)
            scores(1)
            scores(2)
            pe.wait_ge(sem("spread"), 8)
            for q in range(4):
                for i in range(4):
                    mm = pe.transpose(bank(4 + q)[0:NB, i * P:(i + 1) * P], mod3[:, M_G2 + 4 * q + i, 1:9], ident[:])
                mm.then_inc(sem("g2_mm"), 1)
            pe.wait_ge(sem("g2_rows"), 4)
            pe.wait_ge(sem("experts_ready"), 3)
            pe.transpose(bank(0)[:, 0:NB], eidf_s, ident[0:NB, 0:NB])
            pe.transpose(bank(0)[:, NB:2 * NB], bestv[0:NB].rearrange("p h k -> p (h k)"), ident[0:NB, 0:NB]).then_inc(sem("experts_T"), 1)

        def pool_peer(pool):
            c = sem("peer_consts")
            pool.wait_ge(sem("x1_ready"), KD + 1)
            step(pool, c, pool.iota(iota16, [[1, TOPK]], base=0, channel_multiplier=0, allow_small_or_imprecise_dtypes=True))
            step(pool, c, pool.memset(unit, 1.0))
            step(pool, c, pool.affine_select(out=unit, in_=unit, compare_op=ALU.is_equal, fill=0.0, base=0,
                                             pattern=[[1, NB], [-1, NB]], channel_multiplier=0))
            step(pool, c, pool.memset(zrow, 0.0))

        ubuf = [ring[:, j // 2, (j % 2) * D:(j % 2 + 1) * D] for j in range(4)]
        vbuf = [ring[:, 2 + j // 2, (j % 2) * D:(j % 2 + 1) * D] for j in range(4)]
        u_in, v_in = [sem(f"u_in{j}") for j in range(4)], [sem(f"v_in{j}") for j in range(4)]

        def each_slot(eng, t, body, head=None):
            with eng.Fori(0, HEADS // 2) as i:
                for half in range(2):
                    if head:
                        head(i, half)
                    for s in range(TOPK):
                        body(i, half, s, t * SLOTS + half * TOPK + s)

        def pool_gather(pool):
            pool.wait_ge(sem("proj_sum"), 8 + 84)

            def go_on(signal, value):
                pool.wait_ge(sem(signal), value)
                pool.sem_inc(sem("gather_turn"), 1)

            def gather(n0, index, i=None):
                at_n = (lambda k: i * (2 * TOPK) + k) if i is not None else (lambda k: k)
                go_on("dot", at_n(n0 + 1))
                pool.indirect_dma_start(ubuf[n0 % 4], None, io["peer_u"][0], bass.IndirectOffsetOnAxis(index, 0)).then_inc(u_in[n0 % 4], 16)
                go_on("v_used", at_n(n0 + 1))
                pool.indirect_dma_start(vbuf[n0 % 4], None, io["peer_v"][0], bass.IndirectOffsetOnAxis(index, 0)).then_inc(v_in[n0 % 4], 16)

            for t in range(NT):
                pool.wait_ge(sem("experts_ready"), t + 1)

                def head(i, half):
                    h0 = t * HEADS + half
                    pool.tensor_tensor(I32v(idx16[:, half, :]), I32v(eid[:, bass.ds(i * (2 * TOPK) + h0 * TOPK, TOPK)]),
                                       I32v(izero), ALU.add).then_inc(sem("idx_ready"), 1)
                    go_on("idx_ready", i * 2 + (h0 + 1))
                each_slot(pool, t, lambda i, half, s, n0: gather(n0, I32v(idx16[:, half, s:s + 1]), i), head)
            pool.wait_ge(sem("experts_s"), 1)
            for b in range(NB):
                gather(NT * SLOTS + b, I32v(eid_s[:, b:b + 1]))
            for t in range(NT + 1):
                pool.wait_ge(sem("y_ready"), t + 1)
                pool.dma_start(outs["y_prompt"][0, t * P:(t + 1) * P, :] if t < NT else outs["y_sample"].rearrange("b t d -> (b t) d"),
                               x1r[:, t, :] if t < NT else x1s).then_inc(sem("y_out"), 16)
        out_sems.update(y_out=16 * (NT + 1))
        izero = cols("izero", TOPK)

        def dve_experts(dve):
            c = sem("peer_steps")
            step(dve, c, dve.memset(izero, 0.0))
            step(dve, c, dve.tensor_copy(one_row, B2(ident[0:NB, 0:NB], P)))
            dve.wait_ge(sem("peer_consts"), 4)
            for t in range(NT + 1):
                dve_top(dve, t)
            dve.wait_ge(sem("experts_T"), 1)
            step(dve, c, dve.tensor_copy(I32v(eid_s), bank(0)[:, 0:NB]))
            dve.tensor_copy(egate_s, bank(0)[:, NB:2 * NB]).then_inc(sem("experts_s"), 1)
            dve.wait_ge(sem("experts_s"), 1)
            dve.wait_ge(sem("g2_rows"), 4)
            dve.wait_ge(sem("spread"), 8)
            dve.sem_inc(sem("dot"), 4)

            def slot(t, j, h2, column, i_n, i_full):
                dve.wait_ge(u_in[j], i_full)
                dve.scalar_tensor_tensor(products, ubuf[j], 1.0, h2, ALU.mult, ALU.mult, accum_out=dots[:, column:column + 1]).then_inc(sem("dot"), 1)
                dve.wait_ge(sem("gelu"), i_n(1))

            def finish(t):
                r = rows_of[t]
                bk = 4 if t == 1 else 0
                x_, g_ = (x1r[:, t, :], g2B) if t < NT else (x1s, g2s)
                p_ = products[0:r]
                dve.wait_ge(sem("summed"), t + 1)
                step(dve, c, dve.tensor_tensor(v3(products, 0, 4, 512)[0:r], ps[0:r, bk:bk + 4, :], g_[0:r].rearrange("p (a b) -> p a b", b=512), ALU.mult))
                step(dve, sem("x2_ready"), dve.tensor_tensor(x_, x_, p_, ALU.add))
                dve.wait_ge(sem("y_root"), t + 1)
                step(dve, c, dve.reciprocal(yroot[0:r, t:t + 1], yroot[0:r, t:t + 1]))
                dve.scalar_tensor_tensor(x_, x_, yroot[0:r, t:t + 1], fnB[0:r], ALU.mult, ALU.mult).then_inc(sem("y_ready"), 1)

            for t in range(NT):
                def head(i, half):
                    h0 = t * HEADS + half
                    dve.tensor_scalar(gate16[:, half, :], egate[:, bass.ds(i * (2 * TOPK) + h0 * TOPK, TOPK)], 1.0, None, ALU.mult
                                      ).then_inc(sem("gates_here"), 1)
                    dve.wait_ge(sem("gates_here"), i * 2 + (h0 + 1))

                def body(i, half, s, n0):
                    slot(t, n0 % 4, h2r[:, t, :], half * TOPK + s, lambda k: i * 32 + (n0 + k), i * 128 + 16 * (n0 // 4 + 1))
                    dve.wait_ge(sem("v_used"), i * 32 + (n0 + 1))
                    dve.tensor_scalar(diag[:, n0 % 4, :], ident[:], gel[:, half * TOPK + s:half * TOPK + s + 1],
                                      gate16[:, half, s:s + 1], ALU.mult, ALU.mult).then_inc(sem("diag_ready"), 1)
                each_slot(dve, t, body, head)
                finish(t)
            for b in range(NB):
                n = NT * SLOTS + b
                dve.wait_ge(sem("h2_spread"), b + 1)
                dve.wait_ge(u_in[n % 4], 16 * (n // 4 + 1))
                dve.scalar_tensor_tensor(v3(products, 0, 4, 512), ubuf[n % 4].rearrange("p (a b) -> p a b", b=512), 1.0, ps[:, 4:8, :],
                                         ALU.mult, ALU.mult, accum_out=dots[:, b:b + 1]).then_inc(sem("dot"), 1)
                dve.wait_ge(sem("gelu"), n + 1)
                dve.wait_ge(sem("v_used"), n + 3)
                dve.tensor_scalar(wpad[:, b % 2, :], unit[:, b, :], gel[:, b:b + 1], egate_s[:, b:b + 1], ALU.mult, ALU.mult).then_inc(sem("diag_ready"), 1)
            finish(NT)

        def act_experts(act):
            def final_root(t):
                r = rows_of[t]
                act.wait_ge(sem("x2_ready"), t + 1)
                x_ = x1r[:, t, :] if t < NT else x1s
                act.activation(products[0:r], x_, ACT.Square, accum_out=sumsq[0:r, t:t + 1]).then_inc(sem("sumsq"), 1)
                act.wait_ge(sem("sumsq"), t + 1)
                act.activation(yroot[0:r, t:t + 1], sumsq[0:r, t:t + 1], ACT.Sqrt, bias=eps_col[0:r], scale=1.0 / D).then_inc(sem("y_root"), 1)

            for t in range(NT):
                def body(i, half, s, n0):
                    act.wait_ge(sem("dot"), i * 32 + (n0 + 5))
                    act.activation(gel[:, half * TOPK + s:half * TOPK + s + 1], dots[:, half * TOPK + s:half * TOPK + s + 1],
                                   ACT.Gelu_apprx_tanh).then_inc(sem("gelu"), 1)
                each_slot(act, t, body)
                final_root(t)
            for b in range(NB):
                act.wait_ge(sem("dot"), NT * SLOTS + b + 5)
                act.activation(gel[:, b:b + 1], dots[:, b:b + 1], ACT.Gelu_apprx_tanh).then_inc(sem("gelu"), 1)
            final_root(NT)

        def pe_experts(pe):
            pe.sem_inc(sem("v_used"), 4)
            pe.wait_ge(sem("experts_s"), 1)
            pe.wait_ge(sem("proj_sum"), 8 + 84)
            pe.wait_ge(sem("peer_consts"), 4)
            for t in range(NT):
                bk = 4 * t
                for q in range(4):
                    pe.matmul(bank(bk + q), zrow, fnB[0:1, 0:512], start=True, stop=False)

                def body(i, half, s, n0):
                    pe.wait_ge(v_in[n0 % 4], i * 128 + 16 * (n0 // 4 + 1))
                    pe.wait_ge(sem("diag_ready"), i * 32 + (n0 + 1))
                    for q in range(4):
                        mm = pe.matmul(bank(bk + q), diag[:, n0 % 4, :], vbuf[n0 % 4][:, 512 * q:512 * q + 512], start=False, stop=False)
                    mm.then_inc(sem("v_used"), 1)
                each_slot(pe, t, body)
                for q in range(4):
                    mm = pe.matmul(bank(bk + q), zrow, fnB[0:1, 0:512], start=False, stop=True)
                mm.then_inc(sem("summed"), 1)
            for b in range(NB):
                n = NT * SLOTS + b
                if b == 0:
                    pe.wait_ge(sem("x2_ready"), 2)
                pe.wait_ge(sem("dot"), n + 4)
                for q in range(4):
                    mm = pe.matmul(bank(4 + q), one_row[:, b, :], h2s[:, 512 * q:512 * q + 512], start=True, stop=True)
                mm.then_inc(sem("h2_spread"), 1)
                pe.wait_ge(v_in[n % 4], 16 * (n // 4 + 1))
                pe.wait_ge(sem("diag_ready"), n + 1)
                for q in range(4):
                    mm = pe.matmul(bank(q)[0:NB, :], wpad[:, b % 2, :], vbuf[n % 4][:, 512 * q:512 * q + 512], start=b == 0, stop=b == NB - 1)
                mm.then_inc(sem("v_used"), 1)
            pe.wait_ge(sem("v_used"), 4 + NT * SLOTS + NB)
            pe.sem_inc(sem("summed"), 1)




        @block.sync
        def _(sp):
            for stage in (sp_compress, sp_in, sp_delta, sp_w1):
                stage(sp)
            leave(sp, "sp_left")
            for stage in (sp_w2, sp_states_stored, sp_samp, sp_out):
                stage(sp)
            for name, n in out_sems.items():
                sp.wait_ge(sem(name), n)

        @block.scalar
        def _(act):
            for stage in (act_setup, act_compress, act_early, act_in, act_conv, act_delta_gates, act_decay):
                stage(act)
            for j in range(NT):
                act_chunk(act, j)
            act_step(act)
            leave(act, "act_left")
            for stage in (act_kv, act_samp, act_out, act_peer, act_experts):
                stage(act)

        @block.gpsimd
        def _(pool):
            for stage in (pool_setup, pool_att_consts, pool_delta, pool_step, pool_clear, pool_att, pool_samp, pool_peer, pool_gather):
                stage(pool)

        @block.tensor
        def _(pe):
            for stage in (pe_setup, pe_compress, pe_in, pe_delta_norm, pe_delta_gates):
                stage(pe)
            for j in range(NT):
                pe_chunk(pe, j)
            pe_step(pe)
            leave(pe, "pe_left")
            for stage in (pe_kv, pe_samp, pe_out, pe_peer, pe_experts):
                stage(pe)

        @block.vector
        def _(dve):
            for stage in (dve_setup, dve_compress, dve_in, dve_conv, dve_delta_gates):
                stage(dve)
            for j in range(NT):
                dve_chunk(dve, j)
            dve_step(dve)
            leave(dve, "dve_left")
            for stage in (dve_kv, dve_samp, dve_out, dve_experts):
                stage(dve)


_INS = ["x_prompt", "x_sample", "cache_cmp_kv", "cache_sel_kv", "state_win_kv", "state_conv",
        "state_gdn", "page_table", "c_prompt", "c_sample", "w_ada", "b_ada",
        "norm_mix", "norm_ffn", "w_in", "cmp_pe", "cmp_w1", "cmp_b1",
        "cmp_w2", "conv_w", "gdn_a_log", "gdn_dt_bias", "gdn_norm", "w_out",
        "peer_wq", "peer_keys", "peer_u", "peer_v", "final_norm"]
_OUTS = [
    ("y_prompt", (1, 256, 2048)),
    ("y_sample", (8, 1, 2048)),
    ("cmp_p", (1, 1, 256, 2, 2, 128)),
    ("cmp_s", (1, 8, 1, 2, 2, 128)),
    ("sel_p", (1, 1, 256, 2, 2, 128)),
    ("sel_s", (1, 8, 1, 2, 2, 128)),
    ("win_p", (1, 1, 256, 2, 2, 128)),
    ("win_s", (1, 8, 512, 2, 2, 128)),
    ("conv_p", (1, 1, 3, 3072)),
    ("conv_s", (1, 8, 3, 3072)),
    ("gdn_p", (1, 1, 8, 128, 128)),
    ("gdn_s", (1, 8, 8, 128, 128)),
]


def kernel(**inputs):
    import concourse.bacc as bacc
    from concourse.bass_utils import run_bass_kernel_spmd

    nc = bacc.Bacc("TRN2", target_bir_lowering=False, num_devices=1)
    arrays, io, outs = {}, {}, {}
    for name in _INS:
        a = np.ascontiguousarray(inputs[name])
        arrays[f"in_{name}_dram"] = a
        io[name] = nc.dram_tensor(f"in_{name}_dram", a.shape, mybir.dt.from_np(a.dtype), kind="ExternalInput").ap()
    for name, shape in _OUTS:
        outs[name] = nc.dram_tensor(f"out_{name}_dram", shape, F32, kind="ExternalOutput").ap()
    layer_program(nc, io, outs)
    r = run_bass_kernel_spmd(nc, [arrays], core_ids=[0])
    return tuple(r.results[0][f"out_{name}_dram"] for name, _ in _OUTS)
```
